# Optimizing a Trainium2 kernel written in Bass

```python
import math
import jax, jax.numpy as jnp
from jax import lax
import numpy as np

D_MODEL = 1024
BATCH = 1
SEQ = 256
DEPTH = 2

HEAD_DIM = 64
N_HEADS = D_MODEL // HEAD_DIM
MIX_WIDTH = N_HEADS * HEAD_DIM
H_FOX = 5
H_MOBA = 5
H_DIL = N_HEADS - H_FOX - H_MOBA
ROT_DIM = HEAD_DIM // 4
ROPE_THETA = 500000.0
Q_BLOCK = 128
FORGET_BIAS_INIT = 3.0
MOBA_BLOCK = 256
MOBA_TOPK = 3
MOBA_Q_CHUNK = 16
DIL_PATTERNS = ((128, 1), (512, 4), (2048, 16))
BAND_BLOCK = 128
D_FF = 3584
N_EXPERTS = 8
TOP_K = 2
MOE_ROW_BLOCK = 256
EPS = 1e-6

kernel_name = "hymba_fox_moba_dilated_moe"

def rmsnorm(x, g):
    xf = x.astype(jnp.float32)
    y = xf * lax.rsqrt(jnp.mean(xf * xf, axis=-1, keepdims=True) + EPS)
    return (y * g.astype(jnp.float32)).astype(x.dtype)

def rope_tables(seq):
    inv = ROPE_THETA ** (-jnp.arange(0, ROT_DIM, 2, dtype=jnp.float32) / ROT_DIM)
    ang = jnp.arange(seq, dtype=jnp.float32)[:, None] * inv[None, :]
    return jnp.cos(ang), jnp.sin(ang)

def partial_rope(x, cos, sin):
    half = ROT_DIM // 2
    c = cos.astype(x.dtype)
    s = sin.astype(x.dtype)
    x1 = x[..., :half]
    x2 = x[..., half:ROT_DIM]
    return jnp.concatenate([x1 * c - x2 * s, x2 * c + x1 * s, x[..., ROT_DIM:]], axis=-1)

def forgetting_attention(q, k, v, log_f):
    B, H, S, hd = q.shape
    c = jnp.cumsum(log_f, axis=-1)
    scale = hd ** -0.5
    outs = []
    for blk in range(S // Q_BLOCK):
        q0, q1 = blk * Q_BLOCK, (blk + 1) * Q_BLOCK
        logits = jnp.einsum('bhqd,bhkd->bhqk', q[:, :, q0:q1], k[:, :, :q1],
                            preferred_element_type=jnp.float32) * scale
        logits = logits + c[:, :, q0:q1, None] - c[:, :, None, :q1]
        causal = jnp.arange(q0, q1)[:, None] >= jnp.arange(q1)[None, :]
        p = jax.nn.softmax(jnp.where(causal, logits, -jnp.inf), axis=-1)
        outs.append(jnp.einsum('bhqk,bhkd->bhqd', p.astype(v.dtype), v[:, :, :q1]))
    return jnp.concatenate(outs, axis=2)

def moba_attention(q, k, v):
    B, H, S, hd = q.shape
    n_blk = -(-S // MOBA_BLOCK)
    Sp = n_blk * MOBA_BLOCK
    pad = ((0, 0), (0, 0), (0, Sp - S), (0, 0))
    qp, kp, vp = jnp.pad(q, pad), jnp.pad(k, pad), jnp.pad(v, pad)
    k_blocks = kp.reshape(B, H, n_blk, MOBA_BLOCK, hd)
    v_blocks = vp.reshape(B, H, n_blk, MOBA_BLOCK, hd)
    k_mean = jnp.mean(k_blocks.astype(jnp.float32), axis=3).astype(k.dtype)
    topk = min(MOBA_TOPK, n_blk)
    scale = hd ** -0.5
    b_idx = jnp.arange(B)[:, None, None, None]
    h_idx = jnp.arange(H)[None, :, None, None]

    def chunk(ci):
        q0 = ci * MOBA_Q_CHUNK
        qc = lax.dynamic_slice_in_dim(qp, q0, MOBA_Q_CHUNK, axis=2)
        own = q0 // MOBA_BLOCK
        gate = jnp.einsum('bhqd,bhnd->bhqn', qc, k_mean, preferred_element_type=jnp.float32)
        gate = jnp.where(jnp.arange(n_blk) < own, gate, -jnp.inf)
        _, gidx = lax.top_k(gate, topk)
        valid = gidx < own
        ksel = k_blocks[b_idx, h_idx, gidx]
        vsel = v_blocks[b_idx, h_idx, gidx]
        l_sel = jnp.einsum('bhqd,bhqjkd->bhqjk', qc, ksel, preferred_element_type=jnp.float32) * scale
        l_sel = jnp.where(valid[..., None], l_sel, -jnp.inf).reshape(B, H, MOBA_Q_CHUNK, topk * MOBA_BLOCK)
        kown = lax.dynamic_slice_in_dim(kp, own * MOBA_BLOCK, MOBA_BLOCK, axis=2)
        vown = lax.dynamic_slice_in_dim(vp, own * MOBA_BLOCK, MOBA_BLOCK, axis=2)
        l_own = jnp.einsum('bhqd,bhkd->bhqk', qc, kown, preferred_element_type=jnp.float32) * scale
        causal = (q0 + jnp.arange(MOBA_Q_CHUNK))[:, None] >= (own * MOBA_BLOCK + jnp.arange(MOBA_BLOCK))[None, :]
        l_own = jnp.where(causal, l_own, -jnp.inf)
        p = jax.nn.softmax(jnp.concatenate([l_sel, l_own], axis=-1), axis=-1).astype(v.dtype)
        p_sel = p[..., :topk * MOBA_BLOCK].reshape(B, H, MOBA_Q_CHUNK, topk, MOBA_BLOCK)
        p_own = p[..., topk * MOBA_BLOCK:]
        return (jnp.einsum('bhqjk,bhqjkd->bhqd', p_sel, vsel)
                + jnp.einsum('bhqk,bhkd->bhqd', p_own, vown))

    out = lax.map(chunk, jnp.arange(Sp // MOBA_Q_CHUNK))
    return jnp.moveaxis(out, 0, 2).reshape(B, H, Sp, hd)[:, :, :S]

def banded_causal_attention(q, k, v, span):
    *lead, L, hd = q.shape
    nb = -(-L // BAND_BLOCK)
    Lp = nb * BAND_BLOCK
    pad = [(0, 0)] * len(lead) + [(0, Lp - L), (0, 0)]

    def blocks(t):
        return jnp.pad(t, pad).reshape(*lead, nb, BAND_BLOCK, hd)

    def with_prev(t):
        prev = jnp.concatenate([jnp.zeros_like(t[..., :1, :, :]), t[..., :-1, :, :]], axis=-3)
        return jnp.concatenate([prev, t], axis=-2)

    qb = blocks(q)
    kw = with_prev(blocks(k))
    vw = with_prev(blocks(v))
    logits = jnp.einsum('...nqd,...nkd->...nqk', qb, kw, preferred_element_type=jnp.float32) * (hd ** -0.5)
    qpos = (jnp.arange(nb)[:, None] * BAND_BLOCK + jnp.arange(BAND_BLOCK)[None, :])[:, :, None]
    kpos = (jnp.arange(nb)[:, None] * BAND_BLOCK - BAND_BLOCK + jnp.arange(2 * BAND_BLOCK)[None, :])[:, None, :]
    dist = qpos - kpos
    mask = (dist >= 0) & (dist <= span) & (kpos >= 0)
    logits = jnp.where(mask, logits, -jnp.inf)
    lse = jax.nn.logsumexp(logits, axis=-1)
    p = jnp.exp(logits - lse[..., None]).astype(v.dtype)
    out = jnp.einsum('...nqk,...nkd->...nqd', p, vw)
    return out.reshape(*lead, Lp, hd)[..., :L, :], lse.reshape(*lead, Lp)[..., :L]

def dilated_attention(q, k, v):
    B, H, S, hd = q.shape
    outs, lses = [], []
    for window, dil in DIL_PATTERNS:
        L = S // dil

        def to_strided(t):
            return t.reshape(B, H, L, dil, hd).transpose(0, 1, 3, 2, 4)

        o, lse = banded_causal_attention(to_strided(q), to_strided(k), to_strided(v), window // dil)
        outs.append(o.transpose(0, 1, 3, 2, 4).reshape(B, H, S, hd))
        lses.append(lse.transpose(0, 1, 3, 2).reshape(B, H, S))
    w = jax.nn.softmax(jnp.stack(lses, axis=0), axis=0)
    acc = w[0][..., None].astype(q.dtype) * outs[0]
    for i in range(1, len(DIL_PATTERNS)):
        acc = acc + w[i][..., None].astype(q.dtype) * outs[i]
    return acc

def hybrid_mixer(h, w_in, b_f, mix_gain, w_out, cos, sin):
    B, S, _ = h.shape
    proj = h @ w_in
    qkv = proj[..., :3 * MIX_WIDTH].reshape(B, S, 3, N_HEADS, HEAD_DIM).transpose(2, 0, 3, 1, 4)
    q, k, v = qkv[0], qkv[1], qkv[2]
    f_logit = proj[..., 3 * MIX_WIDTH:].astype(jnp.float32) + b_f.astype(jnp.float32)
    log_f = jax.nn.log_sigmoid(f_logit).transpose(0, 2, 1)
    o_a = forgetting_attention(q[:, :H_FOX], k[:, :H_FOX], v[:, :H_FOX], log_f)
    q_r = partial_rope(q[:, H_FOX:], cos, sin)
    k_r = partial_rope(k[:, H_FOX:], cos, sin)
    o_b = moba_attention(q_r[:, :H_MOBA], k_r[:, :H_MOBA], v[:, H_FOX:H_FOX + H_MOBA])
    o_c = dilated_attention(q_r[:, H_MOBA:], k_r[:, H_MOBA:], v[:, H_FOX + H_MOBA:])
    wa, wb = H_FOX * HEAD_DIM, H_MOBA * HEAD_DIM
    ya = rmsnorm(o_a.transpose(0, 2, 1, 3).reshape(B, S, wa), mix_gain[:wa])
    yb = rmsnorm(o_b.transpose(0, 2, 1, 3).reshape(B, S, wb), mix_gain[wa:wa + wb])
    yc = rmsnorm(o_c.transpose(0, 2, 1, 3).reshape(B, S, H_DIL * HEAD_DIM), mix_gain[wa + wb:])
    return jnp.concatenate([ya, yb, yc], axis=-1) @ w_out

def swiglu(h, w1, w3, w2):
    return (jax.nn.silu(h @ w1) * (h @ w3)) @ w2

def moe_swiglu(h, w_router, we1, we3, we2):
    B, S, D = h.shape
    T = B * S
    x = h.reshape(T, D)
    logits = (x @ w_router).astype(jnp.float32)
    top_val, top_idx = lax.top_k(logits, TOP_K)
    gates = jax.nn.softmax(top_val, axis=-1)
    A = T * TOP_K
    expert = top_idx.reshape(A).astype(jnp.int32)
    token = jnp.repeat(jnp.arange(T, dtype=jnp.int32), TOP_K)
    gate = gates.reshape(A)
    order = jnp.argsort(expert)
    e_s, t_s, g_s = expert[order], token[order], gate[order]
    counts = jnp.bincount(expert, length=N_EXPERTS)
    padded = (counts + MOE_ROW_BLOCK - 1) // MOE_ROW_BLOCK * MOE_ROW_BLOCK
    starts = jnp.cumsum(counts) - counts
    pstarts = jnp.cumsum(padded) - padded
    dest = pstarts[e_s] + jnp.arange(A, dtype=jnp.int32) - starts[e_s]
    n_blocks = -(-(A + N_EXPERTS * (MOE_ROW_BLOCK - 1)) // MOE_ROW_BLOCK)
    n_rows = n_blocks * MOE_ROW_BLOCK
    row_token = jnp.full((n_rows,), T, jnp.int32).at[dest].set(t_s)
    row_gate = jnp.zeros((n_rows,), jnp.float32).at[dest].set(g_s)
    block_expert = jnp.minimum(
        jnp.searchsorted(jnp.cumsum(padded), jnp.arange(n_blocks) * MOE_ROW_BLOCK, side='right'),
        N_EXPERTS - 1)
    x_pad = jnp.concatenate([x, jnp.zeros((1, D), x.dtype)], axis=0)

    def body(y, inp):
        tok, g, e = inp
        xb = x_pad[tok]
        hid = jax.nn.silu(xb @ we1[e]) * (xb @ we3[e])
        return y.at[tok].add((hid @ we2[e]) * g[:, None].astype(xb.dtype)), None

    y, _ = lax.scan(body, jnp.zeros_like(x_pad),
                    (row_token.reshape(n_blocks, MOE_ROW_BLOCK),
                     row_gate.reshape(n_blocks, MOE_ROW_BLOCK), block_expert))
    return y[:T].reshape(B, S, D)

def setup_inputs(seed: int = 0) -> dict:
    key = jax.random.key(seed)
    ks = iter(jax.random.split(key, 64))

    def nrm(shape, scale):
        return jax.random.normal(next(ks), shape, jnp.float32) * scale

    def gain(n):
        return 1.0 + nrm((n,), 0.02)

    inp = {"x": nrm((BATCH, SEQ, D_MODEL), 1.0)}
    for l in range(DEPTH):
        p = "l%d_" % l
        inp[p + "norm_mix"] = gain(D_MODEL)
        inp[p + "w_in"] = nrm((D_MODEL, 3 * MIX_WIDTH + H_FOX), D_MODEL ** -0.5)
        inp[p + "b_f"] = FORGET_BIAS_INIT + nrm((H_FOX,), 0.5)
        inp[p + "mix_gain"] = gain(MIX_WIDTH)
        inp[p + "w_out"] = nrm((MIX_WIDTH, D_MODEL), MIX_WIDTH ** -0.5)
        inp[p + "norm_ffn"] = gain(D_MODEL)
        if l % 2 == 0:
            inp[p + "w1"] = nrm((D_MODEL, D_FF), D_MODEL ** -0.5)
            inp[p + "w3"] = nrm((D_MODEL, D_FF), D_MODEL ** -0.5)
            inp[p + "w2"] = nrm((D_FF, D_MODEL), D_FF ** -0.5)
        else:
            inp[p + "w_router"] = nrm((D_MODEL, N_EXPERTS), D_MODEL ** -0.5)
            inp[p + "we1"] = nrm((N_EXPERTS, D_MODEL, D_FF), D_MODEL ** -0.5)
            inp[p + "we3"] = nrm((N_EXPERTS, D_MODEL, D_FF), D_MODEL ** -0.5)
            inp[p + "we2"] = nrm((N_EXPERTS, D_FF, D_MODEL), D_FF ** -0.5)
    inp["final_norm"] = gain(D_MODEL)
    return inp

def reference(x, l0_norm_mix, l0_w_in, l0_b_f, l0_mix_gain, l0_w_out, l0_norm_ffn, l0_w1, l0_w3, l0_w2,
              l1_norm_mix, l1_w_in, l1_b_f, l1_mix_gain, l1_w_out, l1_norm_ffn,
              l1_w_router, l1_we1, l1_we3, l1_we2, final_norm):
    cos, sin = rope_tables(x.shape[1])
    mix_params = [(l0_norm_mix, l0_w_in, l0_b_f, l0_mix_gain, l0_w_out),
                  (l1_norm_mix, l1_w_in, l1_b_f, l1_mix_gain, l1_w_out)]
    ffn_norms = [l0_norm_ffn, l1_norm_ffn]
    ffn_params = [(l0_w1, l0_w3, l0_w2), (l1_w_router, l1_we1, l1_we3, l1_we2)]
    for i in range(DEPTH):
        g_mix, w_in, b_f, mix_gain, w_out = mix_params[i]
        x = x + hybrid_mixer(rmsnorm(x, g_mix), w_in, b_f, mix_gain, w_out, cos, sin)
        h = rmsnorm(x, ffn_norms[i])
        x = x + (swiglu(h, *ffn_params[i]) if i % 2 == 0 else moe_swiglu(h, *ffn_params[i]))
    return rmsnorm(x, final_norm)


_drawn_inputs = setup_inputs


def setup_inputs(seed=0):
    import zlib

    import numpy as np

    out = dict(_drawn_inputs(seed))
    spreads = {}
    factors = {'l1_norm_mix': 2.827, 'l1_norm_ffn': 2.845, 'final_norm': 2.986}
    for name, (base, spread) in spreads.items():
        noise = np.random.default_rng([zlib.crc32(name.encode()), seed]).standard_normal(out[name].shape)
        drawn = base * np.exp(spread * noise) if base else spread * noise
        out[name] = __import__('jax').numpy.asarray(drawn.astype(out[name].dtype))
    for name, factor in factors.items():
        out[name] = (out[name] * factor).astype(out[name].dtype)
    return out
```

```python
import concourse.bass as bass
from concourse import mybir
from contextlib import ExitStack

F32 = mybir.dt.float32
I32 = mybir.dt.int32
U32 = mybir.dt.uint32
ALU = mybir.AluOpType
ACT = mybir.ActivationFunctionType
AX = mybir.AxisListType.X

P = 128
D = 1024
S = 256
HD = 64
NH = 16
H_FOX = 5
H_MOBA = 5
F = 3584
NE = 8
EPS = 1e-6
TT = S // P
KD = D // P
ROT = HD // 4
HALF = ROT // 2
GROUP = 256
CH = GROUP // P
NG = F // GROUP
RING_SLOTS = 14
TILE = KD * GROUP
PER_FFN = 3 * NG
MIX_TILES = 16
CAP = 128
NARROW = (64, 96)
TRI = 3 * P
GROUPS = ((0, H_FOX * HD), (H_FOX * HD, (H_FOX + H_MOBA) * HD), ((H_FOX + H_MOBA) * HD, D))

C_ID, C_LT, C_ONE, C_IOTA = 0, 128, 256, 384
C_CAUSAL, C_UNION, C_MULT = 512, 512 + TRI, 512 + 2 * TRI
C_COS = 512 + 3 * TRI
C_SIN = C_COS + TT * HALF
C_SEL = C_SIN + TT * HALF
C_END = C_SEL + H_FOX * P


def up_tile(g):
    return 0 if g == 0 else 3 * g - 1


def down_tile(g):
    return 3 * g + 4 if g < NG - 1 else PER_FFN - 1


def ffn_order():
    order = [None] * PER_FFN
    for g in range(NG):
        order[up_tile(g)] = ("w1", g)
        order[up_tile(g) + 1] = ("w3", g)
        order[down_tile(g)] = ("w2", g)
    return order


def hybrid_trunk(nc, a, out):
    ctx = ExitStack()
    with ctx:
        def sb(name, shape, dt=F32):
            return ctx.enter_context(nc.sbuf_tensor(name, shape, dt))

        def sem(name):
            return ctx.enter_context(nc.semaphore(name))

        ring = sb("ring", [P, RING_SLOTS, TILE])
        const = sb("const", [P, C_END])
        x = sb("x_res", [P, TT, D])
        h = sb("h_tok", [P, TT, D])
        hT = sb("h_T", [P, KD, S])
        gain = sb("gain", [P, 2, D])
        work = sb("work", [P, TT * 3 * D + 2 * KD * S])
        act_buf = sb("act_buf", [P, 4, CH * S])
        wf = sb("w_forget", [P, KD, H_FOX])
        bf = sb("b_forget", [H_FOX, 1])
        wr = sb("w_router", [P, KD, NE])
        small = sb("small", [P, 512])
        fox = sb("fox_rows", [H_FOX, 3, S])
        idx8 = sb("idx8", [P, TT, 8], U32)
        counts = sb("counts", [1, 16], I32)

        ident = const[:, C_ID:C_ID + P]
        before = const[:, C_LT:C_LT + P]
        ones = const[:, C_ONE:C_ONE + P]
        iota = const[:, C_IOTA:C_IOTA + P]
        qkv = work[:, 0:TT * 3 * D].rearrange("p (t n) -> p t n", t=TT)
        qkT = work[:, TT * 3 * D:].rearrange("p (c t) -> p c t", c=2 * KD)
        o_tok = qkv[:, :, 0:D]
        fox_bias = h[:, :, :].rearrange("p t d -> p (t d)")[:, 0:H_FOX * TRI].rearrange("p (h n) -> p h n", h=H_FOX)
        probs = act_buf[:, 0:2, 0:TRI]
        probsT = act_buf[:, 2:4, 0:TRI]
        o = 0
        pick = work[:, o:o + (NE + 1) * TT * CAP].rearrange("p (e t c) -> p e t c", e=NE + 1, t=TT)
        o += (NE + 1) * TT * CAP
        hg = work[:, o:o + 2 * KD * CAP].rearrange("p (b k c) -> p b k c", b=2, k=KD)
        o += 2 * KD * CAP
        gated = work[:, o:o + TT * CAP].rearrange("p (t c) -> p t c", t=TT)
        o += TT * CAP
        spread = work[:, o:o + S]
        o += S
        y_sb = work[:, o:o + D]
        sil = act_buf[:, 0:2, :]
        hid = act_buf[:, 2:4, :]
        ss = small[:, 0:8]
        rstd = small[:, 8:16]
        newton = small[:, 306:314]
        negmax = small[:, 16:48].rearrange("p (h t) -> p h t", t=TT)
        rowmax = small[:, 48:80].rearrange("p (h t) -> p h t", t=TT)
        rowsum = small[:, 80:112].rearrange("p (t h) -> p t h", t=TT)
        rinv = small[:, 112:144].rearrange("p (t h) -> p t h", t=TT)
        cT = small[:, 144:144 + TT * H_FOX].rearrange("p (t h) -> p t h", t=TT)
        lg = small[:, 160:176].rearrange("p (t e) -> p t e", t=TT)
        top = small[:, 176:192].rearrange("p (t e) -> p t e", t=TT)
        idf = small[:, 192:208].rearrange("p (t e) -> p t e", t=TT)
        pick0 = small[:, 208:224].rearrange("p (t e) -> p t e", t=TT)
        pick1 = small[:, 224:240].rearrange("p (t e) -> p t e", t=TT)
        mask = small[:, 240:256].rearrange("p (t e) -> p t e", t=TT)
        gate = small[:, 256:272].rearrange("p (t e) -> p t e", t=TT)
        pos = small[:, 272:288].rearrange("p (t e) -> p t e", t=TT)
        dz = small[:, 288:290]
        z = small[:, 290:292]
        den = small[:, 292:294]
        g0 = small[:, 294:296]
        g1 = small[:, 296:298]
        cnt_f = small[0:1, 298:306]
        rope_t = small[:, 320:496]

        bank = [ctx.enter_context(nc.psum_tensor(f"bank{i}", [P, 512], F32)) for i in range(8)]

        const_in, x_in, small_in = sem("const_in"), sem("x_in"), sem("small_in")
        wf_in = sem("wf_in")
        gain_in = [sem(f"gain_in{i}") for i in range(2)]
        tile_in = [sem(f"tile_in{i}") for i in range(RING_SLOTS)]
        tile_used = sem("tile_used")
        h_ready = sem("h_ready")
        y_ready = sem("y_ready")
        var_ready, root_ready = sem("var_ready"), sem("root_ready")
        tr_done = sem("tr_done")
        hT_by_act, hT_by_dve = sem("hT_by_act"), sem("hT_by_dve")
        forget_done, forget_ln, c_ready = sem("forget_done"), sem("forget_ln"), sem("c_ready")
        proj_copied = sem("proj_copied")
        bias_done, bias_ready = sem("bias_done"), sem("bias_ready")
        rope_ready = sem("rope_ready")
        qk_tr_done, qkT_by_act, qkT_by_dve = sem("qk_tr_done"), sem("qkT_by_act"), sem("qkT_by_dve")
        scores_done, logits_ready, exp_done, weighted = (sem("scores_done"), sem("logits_ready"),
                                                         sem("exp_done"), sem("weighted"))
        probs_tr_done, probsT_ready, pv_done, o_ready = (sem("probs_tr_done"), sem("probsT_ready"),
                                                         sem("pv_done"), sem("o_ready"))
        silu_done, hid_done = sem("silu_done"), sem("hid_done")
        router_done, top_ready, z_ready, mask_ready = (sem("router_done"), sem("top_ready"),
                                                       sem("z_ready"), sem("mask_ready"))
        pos_done, counts_ready = sem("pos_done"), sem("counts_ready")
        pick_ready = sem("pick_ready")
        gather_done, hg_ready = sem("gather_done"), sem("hg_ready")
        scatter_done, scatter_added = sem("scatter_done"), sem("scatter_added")
        gated_ready, spread_done, spread_ready = sem("gated_ready"), sem("spread_done"), sem("spread_ready")
        y_copied = sem("y_copied")
        out_ready, out_stored = sem("out_ready"), sem("out_stored")
        act_chain = sem("act_chain")
        dve_chain, dve_chain_pass, dve_chain_end = sem("dve_chain"), sem("dve_chain_pass"), sem("dve_chain_end")

        def linker(eng, s):
            n = [0]

            def link(ins):
                n[0] += 1
                ins.then_inc(s, 1)
                eng.wait_ge(s, n[0])
            return link

        MIX0 = (0, MIX_TILES + PER_FFN)
        FFN0 = (MIX_TILES, 2 * MIX_TILES + PER_FFN)

        def slot(n):
            return ring[:, n % RING_SLOTS, :]

        def await_tile(eng, n, trip=0):
            eng.wait_ge(tile_in[n % RING_SLOTS], 16 * (n // RING_SLOTS + 1) + trip * (16 * (PER_FFN // RING_SLOTS)))

        def moe_trip(pass_no, e):
            return e + NE * pass_no

        block = ctx.enter_context(nc.Block())

        @block.sync
        def _(sp):
            def load(n, src, trip=None):
                if n >= RING_SLOTS:
                    need = n - RING_SLOTS + 1
                    sp.wait_ge(tile_used, need if trip is None else trip * PER_FFN + need)
                shaped = slot(n).rearrange("p (k c) -> p k c", k=src.shape[1])
                sp.dma_start(shaped, src).then_inc(tile_in[n % RING_SLOTS], 16)

            def swiglu_src(kind, g, w1, w3, w2):
                if kind == "w2":
                    return w2[g * GROUP:(g + 1) * GROUP, :].rearrange("(c p) n -> p c n", p=P)
                w = w1 if kind == "w1" else w3
                return w[:, g * GROUP:(g + 1) * GROUP].rearrange("(k p) n -> p k n", p=P)

            sp.dma_start(x[:, :, :], a["x"].rearrange("b (t p) d -> p (b t) d", p=P)).then_inc(x_in, 16)
            sp.dma_start(const[:, :], a["const"]).then_inc(const_in, 16)
            sp.dma_start(wf[:, :, :], a["l0_w_in"][:, 3 * D:].rearrange("(k p) n -> p k n", p=P)).then_inc(wf_in, 16)
            sp.dma_start(bf[:, :], a["l0_b_f"].rearrange("(h o) -> h o", o=1)).then_inc(wf_in, 16)
            sp.dma_start(wr[:, :, :], a["l1_w_router"].rearrange("(k p) n -> p k n", p=P)).then_inc(small_in, 16)
            for layer in range(2):
                n = MIX0[layer]
                for name, width in (("w_in", 3 * D), ("w_out", D)):
                    w = a[f"l{layer}_{name}"]
                    for c in range(width // GROUP):
                        load(n, w[:, c * GROUP:(c + 1) * GROUP].rearrange("(k p) n -> p k n", p=P))
                        n += 1
                        if layer == 0 and name == "w_out" and c == 3:
                            sp.wait_ge(c_ready, 1)
                            sp.dma_start(wf[:, :, :], a["l1_w_in"][:, 3 * D:].rearrange("(k p) n -> p k n", p=P)
                                         ).then_inc(wf_in, 16)
                            sp.dma_start(bf[:, :], a["l1_b_f"].rearrange("(h o) -> h o", o=1)).then_inc(wf_in, 16)
                if layer == 0:
                    for j, (kind, g) in enumerate(ffn_order()):
                        load(FFN0[0] + j, swiglu_src(kind, g, a["l0_w1"], a["l0_w3"], a["l0_w2"]))

            def experts(pass_no):
                with sp.Fori(0, NE) as e:
                    ws = [a[k][bass.ds(e, 1), :, :].rearrange("e r c -> (e r) c") for k in ("l1_we1", "l1_we3", "l1_we2")]
                    for j, (kind, g) in enumerate(ffn_order()):
                        load(FFN0[1] + j, swiglu_src(kind, g, *ws), moe_trip(pass_no, e))

            experts(0)
            sp.wait_ge(counts_ready, 1)
            most = sp.value_load(counts[0:1, NE:NE + 1], min_val=0, max_val=S)
            with sp.If(most > CAP):
                experts(1)
                sp.nop()
            for t in range(TT):
                sp.wait_ge(out_ready, t + 1)
                sp.dma_start(out[0, t * P:(t + 1) * P, :], h[:, t, :]).then_inc(out_stored, 16)
            sp.wait_ge(out_stored, 16 * TT)

        @block.gpsimd
        def _(pool):
            order = ("l0_norm_mix", "l0_mix_gain", "l0_norm_ffn", "l1_norm_mix", "l1_mix_gain", "l1_norm_ffn",
                     "final_norm")
            freed = ((h_ready, 2), (y_ready, 2), (h_ready, 4), (h_ready, 6), (y_ready, 4))
            for i, name in enumerate(order):
                if i >= 2:
                    pool.wait_ge(*freed[i - 2])
                pool.dma_start(gain[:, i % 2, :], a[name].partition_broadcast(P)).then_inc(gain_in[i % 2], 16)

        @block.scalar
        def _(act):
            link = linker(act, act_chain)

            def copy_transposed(stage):
                for i, b in enumerate((0, 2)):
                    act.wait_ge(tr_done, 4 * stage + b + 1)
                    act.copy(hT[:, 2 * b:2 * b + 2, :], bank[4 + b][:, :].rearrange("p (k t) -> p k t", k=2)
                             ).then_inc(hT_by_act, 1)

            def root(norm_no, n):
                act.wait_ge(var_ready, norm_no + 1)
                link(act.activation(rstd[:, 0:n], ss[:, 0:n], ACT.Ln))
                act.activation(rstd[:, 0:n], rstd[:, 0:n], ACT.Exp, scale=-0.5).then_inc(root_ready, 1)

            def mixer(layer):
                root(3 * layer, TT)
                copy_transposed(3 * layer)
                act.wait_ge(forget_done, layer + 1)
                link(act.activation(fox[:, 0, :], bank[4][0:H_FOX, 0:S], ACT.Identity, bias=bf[:, :]))
                link(act.activation(fox[:, 1, :], fox[:, 0, :], ACT.Abs))
                link(act.activation(fox[:, 1, :], fox[:, 1, :], ACT.Exp, scale=-1.0))
                act.activation(fox[:, 1, :], fox[:, 1, :], ACT.Ln, bias=1.0).then_inc(forget_ln, 1)
                for c in range(6):
                    act.wait_ge(tile_used, MIX0[layer] + 2 * c + 2)
                    for t in range(TT):
                        act.activation(qkv[:, t, c * 512:(c + 1) * 512], bank[2 * (c % 2) + t][:, :], ACT.Copy,
                                       scale=(HD ** -0.5 if c < 2 else 1.0)).then_inc(proj_copied, 1)
                for f in range(0, 8, 2):
                    act.wait_ge(qk_tr_done, 8 * layer + f + 1)
                    act.copy(qkT[:, 2 * f:2 * f + 2, :], bank[4 + f % 4][:, :].rearrange("p (c t) -> p c t", c=2)
                             ).then_inc(qkT_by_act, 1)

                def exps(hh):
                    act.wait_ge(logits_ready, NH * layer + hh + 1)
                    for t in range(TT):
                        lo, hi = (0, P) if t == 0 else (P, TRI)
                        row = probs[:, hh % 2, lo:hi]
                        ins = act.activation(row, row, ACT.Exp, bias=negmax[:, hh, t:t + 1],
                                             accum_out=rowsum[:, t, hh:hh + 1])
                    ins.then_inc(exp_done, 1)

                exps(0)
                for hh in range(NH):
                    if hh + 1 < NH:
                        exps(hh + 1)
                    act.wait_ge(probs_tr_done, NH * layer + hh + 1)
                    if hh >= 2:
                        act.wait_ge(pv_done, NH * layer + hh - 1)
                    act.copy(probsT[:, hh % 2, :], bank[2 + hh % 2][:, 0:TRI]).then_inc(probsT_ready, 1)
                root(3 * layer + 1, 3 * TT)
                copy_transposed(3 * layer + 1)

            def silu(G, b, n, cols, trip=0):
                act.wait_ge(tile_used, n + 1 + trip * PER_FFN)
                if G >= 2:
                    act.wait_ge(hid_done, G - 1 + trip * NG)
                act.activation(sil[:, b, 0:CH * cols], bank[b][:, 0:CH * cols], ACT.Silu).then_inc(silu_done, 1)

            mixer(0)
            root(2, TT)
            copy_transposed(2)
            for g in range(NG):
                silu(g, g % 2, FFN0[0] + up_tile(g), S)
            mixer(1)
            root(5, TT)
            copy_transposed(5)
            act.wait_ge(top_ready, 1)
            act.activation(z, dz, ACT.Exp).then_inc(z_ready, 1)
            for half in range(2):
                act.mul(y_sb[:, half * 512:(half + 1) * 512], const[:, half * 512:(half + 1) * 512], 0.0
                        ).then_inc(y_copied, 1)

            def experts(pass_no):
                with act.Fori(0, NE) as e:
                    trip = moe_trip(pass_no, e)
                    for g in range(NG):
                        silu(NG + g, g % 2, FFN0[1] + up_tile(g), CAP, trip)
                    act.wait_ge(tile_used, FFN0[1] + PER_FFN + trip * PER_FFN)
                    for half in range(2):
                        act.copy(y_sb[:, half * 512:(half + 1) * 512], bank[4 + half][:, :]).then_inc(y_copied, 1)

            experts(0)
            act.wait_ge(counts_ready, 1)
            most = act.value_load(counts[0:1, NE:NE + 1], min_val=0, max_val=S)
            with act.If(most > CAP):
                experts(1)
                act.nop()
            root(6, TT)

        @block.vector
        def _(dve):
            link = linker(dve, dve_chain)

            def await_gain(i):
                dve.wait_ge(gain_in[i % 2], 16 * (i // 2 + 1))
                return gain[:, i % 2, :]

            def inverse_root(norm_no, n, link):
                dve.tensor_scalar(ss[:, 0:n], ss[:, 0:n], EPS, None, ALU.add).then_inc(var_ready, 1)
                dve.wait_ge(root_ready, norm_no + 1)
                link(dve.tensor_tensor(newton[:, 0:n], rstd[:, 0:n], rstd[:, 0:n], ALU.mult))
                link(dve.tensor_tensor(newton[:, 0:n], newton[:, 0:n], ss[:, 0:n], ALU.mult))
                link(dve.tensor_scalar(newton[:, 0:n], newton[:, 0:n], -0.5, 1.5, ALU.mult, ALU.add))
                link(dve.tensor_tensor(rstd[:, 0:n], rstd[:, 0:n], newton[:, 0:n], ALU.mult))

            def norm(gain_no, done, link):
                for t in range(TT):
                    link(dve.tensor_tensor_reduce(out=h[:, t, :], in0=x[:, t, :], in1=x[:, t, :], scale=1.0 / D, scalar=0.0,
                                                  op0=ALU.mult, op1=ALU.add, accum_out=ss[:, t:t + 1]))
                inverse_root(gain_no, TT, link)
                g = await_gain(gain_no)
                for t in range(TT):
                    dve.scalar_tensor_tensor(out=h[:, t, :], in0=x[:, t, :], scalar=rstd[:, t:t + 1], in1=g,
                                             op0=ALU.mult, op1=ALU.mult).then_inc(done, 1)

            def copy_transposed(stage):
                for b in (1, 3):
                    dve.wait_ge(tr_done, 4 * stage + b + 1)
                    dve.tensor_copy(hT[:, 2 * b:2 * b + 2, :], bank[4 + b][:, :].rearrange("p (k t) -> p k t", k=2)
                                    ).then_inc(hT_by_dve, 1)

            def mixer(layer):
                norm(3 * layer, h_ready, link)
                copy_transposed(3 * layer)
                dve.wait_ge(forget_ln, layer + 1)
                link(dve.tensor_scalar(fox[:, 0, :], fox[:, 0, :], 0.0, None, ALU.min))
                link(dve.tensor_tensor(fox[:, 1, :], fox[:, 0, :], fox[:, 1, :], ALU.subtract))
                link(dve.tensor_scalar(fox[:, 2, :], fox[:, 1, :], 0.0, 1.0, ALU.mult, ALU.add))
                link(dve.tensor_tensor_scan(fox[:, 0, :], fox[:, 2, :], fox[:, 1, :], 0.0, ALU.mult, ALU.add))
                dve.tensor_scalar(fox[:, 1, :], fox[:, 0, :], -1.0, None, ALU.mult).then_inc(c_ready, 1)
                dve.wait_ge(bias_done, layer + 1)
                link(dve.tensor_copy(cT, bank[4][:, 0:TT * H_FOX].rearrange("p (t h) -> p t h", t=TT)))
                for hh in range(H_FOX):
                    src = bank[5 + hh // 2][:, (hh % 2) * S:(hh % 2 + 1) * S]
                    for t in range(TT):
                        lo, hi = (0, P) if t == 0 else (P, TRI)
                        link(dve.scalar_tensor_tensor(out=fox_bias[:, hh, lo:hi], in0=src[:, 0:hi - lo],
                                                      scalar=cT[:, t, hh:hh + 1],
                                                      in1=const[:, C_CAUSAL + lo:C_CAUSAL + hi],
                                                      op0=ALU.add, op1=ALU.add))
                dve.sem_inc(bias_ready, 1)
                dve.wait_ge(proj_copied, 12 * layer + 8)
                for t in range(TT):
                    qk = qkv[:, t, 0:2 * D].rearrange("p (s h d) -> p s h d", s=2, h=NH)[:, :, H_FOX:, :]
                    n = NH - H_FOX
                    for s in range(2):
                        x1, x2 = qk[:, s, :, 0:HALF], qk[:, s, :, HALF:ROT]
                        cs = const[:, C_COS + t * HALF:C_COS + (t + 1) * HALF].unsqueeze(1).to_broadcast([P, n, HALF])
                        sn = const[:, C_SIN + t * HALF:C_SIN + (t + 1) * HALF].unsqueeze(1).to_broadcast([P, n, HALF])
                        ta = rope_t[:, 0:n * HALF].rearrange("p (h d) -> p h d", h=n)
                        tb = rope_t[:, n * HALF:2 * n * HALF].rearrange("p (h d) -> p h d", h=n)
                        link(dve.tensor_tensor(ta, x2, sn, ALU.mult))
                        link(dve.tensor_tensor(tb, x1, sn, ALU.mult))
                        link(dve.tensor_tensor(x1, x1, cs, ALU.mult))
                        link(dve.tensor_tensor(x2, x2, cs, ALU.mult))
                        link(dve.tensor_tensor(x1, x1, ta, ALU.subtract))
                        link(dve.tensor_tensor(x2, x2, tb, ALU.add))
                    dve.sem_inc(rope_ready, 1)
                for f in range(1, 8, 2):
                    dve.wait_ge(qk_tr_done, 8 * layer + f + 1)
                    dve.tensor_copy(qkT[:, 2 * f:2 * f + 2, :], bank[4 + f % 4][:, :].rearrange("p (c t) -> p c t", c=2)
                                    ).then_inc(qkT_by_dve, 1)

                def logits(hh):
                    dve.wait_ge(scores_done, NH * layer + hh + 1)
                    if hh >= 2:
                        dve.wait_ge(probs_tr_done, NH * layer + hh - 1)
                    if hh < H_FOX:
                        bias = fox_bias[:, hh, :]
                    else:
                        c0 = C_CAUSAL if hh < H_FOX + H_MOBA else C_UNION
                        bias = const[:, c0:c0 + TRI]
                    for t in range(TT):
                        lo, hi = (0, P) if t == 0 else (P, TRI)
                        ins = dve.tensor_tensor_reduce(out=probs[:, hh % 2, lo:hi], in0=bank[hh % 2][:, lo:hi],
                                                       in1=bias[:, lo:hi], scale=1.0, scalar=-3.0e38, op0=ALU.add,
                                                       op1=ALU.max, accum_out=rowmax[:, hh, t:t + 1])
                        link(ins)
                    dve.tensor_scalar(negmax[:, hh, :], rowmax[:, hh, :], -1.0, None, ALU.mult
                                      ).then_inc(logits_ready, 1)

                logits(0)
                for hh in range(NH):
                    if hh + 1 < NH:
                        logits(hh + 1)
                    if hh >= H_FOX + H_MOBA:
                        dve.wait_ge(exp_done, NH * layer + hh + 1)
                        for t in range(TT):
                            lo, hi = (0, P) if t == 0 else (P, TRI)
                            row = probs[:, hh % 2, lo:hi]
                            ins = dve.tensor_tensor_reduce(out=row, in0=row, in1=const[:, C_MULT + lo:C_MULT + hi],
                                                           scale=1.0, scalar=0.0, op0=ALU.mult, op1=ALU.add,
                                                           accum_out=rowsum[:, t, hh:hh + 1])
                            if t == 0:
                                link(ins)
                        ins.then_inc(weighted, 1)
                    if hh % 4 == 3:
                        q4 = hh // 4
                        dve.wait_ge(pv_done, NH * layer + hh + 1)
                        link(dve.reciprocal(rinv[:, :, 4 * q4:4 * q4 + 4], rowsum[:, :, 4 * q4:4 * q4 + 4]))
                        src = bank[4 + q4 % 2][:, :].rearrange("p (t h d) -> p t h d", t=TT, h=4)
                        for t in range(TT):
                            link(dve.tensor_tensor(
                                o_tok[:, t, q4 * 4 * HD:(q4 + 1) * 4 * HD].rearrange("p (h d) -> p h d", h=4),
                                src[:, t, :, :],
                                rinv[:, t, 4 * q4:4 * q4 + 4].unsqueeze(2).to_broadcast([P, 4, HD]), ALU.mult))
                        dve.sem_inc(o_ready, 1)
                for t in range(TT):
                    for i, (lo, hi) in enumerate(GROUPS):
                        link(dve.tensor_tensor_reduce(out=h[:, t, lo:hi], in0=o_tok[:, t, lo:hi],
                                                      in1=o_tok[:, t, lo:hi], scale=1.0 / (hi - lo), scalar=0.0,
                                                      op0=ALU.mult, op1=ALU.add,
                                                      accum_out=ss[:, 3 * t + i:3 * t + i + 1]))
                inverse_root(3 * layer + 1, 6, link)
                gm = await_gain(3 * layer + 1)
                for t in range(TT):
                    for i, (lo, hi) in enumerate(GROUPS):
                        ins = dve.scalar_tensor_tensor(out=h[:, t, lo:hi], in0=o_tok[:, t, lo:hi],
                                                       scalar=rstd[:, 3 * t + i:3 * t + i + 1], in1=gm[:, lo:hi],
                                                       op0=ALU.mult, op1=ALU.mult)
                        if i < 2:
                            link(ins)
                    ins.then_inc(y_ready, 1)
                copy_transposed(3 * layer + 1)
                for half in range(2):
                    dve.wait_ge(tile_used, MIX0[layer] + 12 + 2 * half + 2)
                    for t in range(TT):
                        xs = x[:, t, half * 512:(half + 1) * 512]
                        link(dve.tensor_tensor(xs, xs, bank[2 * half + t][:, :], ALU.add))

            def hidden(b, G, n, cols, trip=0):
                dve.wait_ge(silu_done, G + 1 + trip * NG)
                dve.wait_ge(tile_used, n + 2 + trip * PER_FFN)
                dve.tensor_tensor(hid[:, b, 0:CH * cols], sil[:, b, 0:CH * cols], bank[2 + b][:, 0:CH * cols], ALU.mult
                                  ).then_inc(hid_done, 1)

            dve.wait_ge(x_in, 16)
            dve.wait_ge(const_in, 16)
            mixer(0)
            norm(2, h_ready, link)
            copy_transposed(2)
            for g in range(NG):
                hidden(g % 2, g, FFN0[0] + up_tile(g), S)
            dve.wait_ge(tile_used, FFN0[0] + PER_FFN)
            for t in range(TT):
                for half in range(2):
                    xs = x[:, t, half * 512:(half + 1) * 512]
                    link(dve.tensor_tensor(xs, xs, bank[4 + 2 * t + half][:, :], ALU.add))
            mixer(1)
            norm(5, h_ready, link)
            copy_transposed(5)

            dve.wait_ge(router_done, 1)
            link(dve.tensor_copy(lg, bank[4][:, 0:TT * NE].rearrange("p (t e) -> p t e", t=TT)))
            for t in range(TT):
                link(dve.max(top[:, t, :], lg[:, t, :]))
                link(dve.max_index(idx8[:, t, :], top[:, t, :], lg[:, t, :]))
            link(dve.tensor_copy(idf, idx8[:, :, :]))
            dve.tensor_tensor(dz, top[:, :, 1], top[:, :, 0], ALU.subtract).then_inc(top_ready, 1)
            for t in range(TT):
                link(dve.tensor_scalar(pick0[:, t, :], iota[:, 0:NE], idf[:, t, 0:1], None, ALU.is_equal))
                link(dve.tensor_scalar(pick1[:, t, :], iota[:, 0:NE], idf[:, t, 1:2], None, ALU.is_equal))
            dve.tensor_tensor(mask, pick0, pick1, ALU.add).then_inc(mask_ready, 1)
            dve.wait_ge(mask_ready, 1)
            dve.wait_ge(z_ready, 1)
            link(dve.tensor_scalar(den, z, 1.0, None, ALU.add))
            link(dve.reciprocal(g0, den))
            link(dve.tensor_tensor(g1, z, g0, ALU.mult))
            for t in range(TT):
                link(dve.tensor_scalar(gate[:, t, :], pick0[:, t, :], g0[:, t:t + 1], None, ALU.mult))
                link(dve.scalar_tensor_tensor(out=gate[:, t, :], in0=pick1[:, t, :], scalar=g1[:, t:t + 1],
                                              in1=gate[:, t, :], op0=ALU.mult, op1=ALU.add))
            dve.wait_ge(pos_done, 1)
            link(dve.scalar_tensor_tensor(out=pos, in0=bank[5][:, 0:TT * NE].rearrange("p (t e) -> p t e", t=TT),
                                          scalar=1.0, in1=mask, op0=ALU.add, op1=ALU.mult))
            link(dve.tensor_scalar(pos, pos, -1.0, None, ALU.add))
            link(dve.tensor_copy(counts[0:1, 0:NE], bank[6][0:1, 0:NE]))
            link(dve.tensor_reduce(cnt_f[0:1, 0:1], bank[6][0:1, 0:NE], AX, ALU.max))
            dve.tensor_copy(counts[0:1, NE:NE + 1], cnt_f[0:1, 0:1]).then_inc(counts_ready, 1)

            def experts(pass_no, link):
                if pass_no:
                    link(dve.tensor_scalar(pos, pos, float(-CAP), None, ALU.add))
                link(dve.memset(pick[:, NE, :, :], 0.0))
                for t in range(TT):
                    link(dve.tensor_tensor(pick[:, 0:NE, t, :], iota.unsqueeze(1).to_broadcast([P, NE, CAP]),
                                           pos[:, t, :].unsqueeze(2).to_broadcast([P, NE, CAP]), ALU.is_equal))
                dve.sem_inc(pick_ready, 1)
                dve.memset(spread, 0.0).then_inc(spread_ready, 1)

                def take_gathered(i, b):
                    for half in range(2):
                        dve.wait_ge(gather_done, 2 * i + half + 1)
                        src = bank[6 + half][:, :].rearrange("p (k c) -> p k c", k=KD // 2)
                        if isinstance(b, int):
                            dst = hg[:, b, half * 4:half * 4 + 4, :]
                        else:
                            dst = hg[:, bass.ds(b, 1), half * 4:half * 4 + 4, :].rearrange("p b k c -> p (b k) c")
                        dve.tensor_copy(dst, src).then_inc(hg_ready, 1)

                def add_scattered(i):
                    for item in range(4):
                        t, half = item // 2, item % 2
                        dve.wait_ge(scatter_done, 4 * i + item + 1)
                        xs = x[:, t, half * 512:(half + 1) * 512]
                        dve.tensor_tensor(xs, xs, bank[6 + item % 2][:, :], ALU.add).then_inc(scatter_added, 1)

                take_gathered((NE + 1) * pass_no, 0)
                with dve.Fori(0, NE) as e:
                    trip = moe_trip(pass_no, e)
                    i = e + (NE + 1) * pass_no
                    for g in range(NG):
                        hidden(g % 2, NG + g, FFN0[1] + up_tile(g), CAP, trip)
                        if g == 0:
                            add_scattered(i)
                        if g == 3:
                            for t in range(TT):
                                ins = dve.tensor_scalar(
                                    gated[:, t, :], pick[:, bass.ds(e, 1), t, :].rearrange("p e c -> p (e c)"),
                                    gate[:, t, bass.ds(e, 1)], None, ALU.mult)
                                ins.then_inc(gated_ready, 1)
                        if g == 6:
                            dve.wait_ge(spread_done, trip + 1)
                            dve.tensor_copy(spread, bank[6][:, 0:S]).then_inc(spread_ready, 1)
                        if g == 9:
                            take_gathered(i + 1, (e + 1) % 2)
                add_scattered((NE + 1) * pass_no + NE)

            experts(0, link)
            dve.wait_ge(scatter_added, 4 * (NE + 1))
            most = dve.value_load(counts[0:1, NE:NE + 1], min_val=0, max_val=S)
            with dve.If(most > CAP):
                experts(1, linker(dve, dve_chain_pass))
                dve.wait_ge(scatter_added, 8 * (NE + 1))
                dve.nop()
            norm(6, out_ready, linker(dve, dve_chain_end))

        @block.tensor
        def _(pe):
            def transpose_tokens(stage, ready, value):
                for t in range(TT):
                    pe.wait_ge(ready, value + t + 1)
                    for k in range(KD):
                        c0 = (k % 2) * S + t * P
                        ins = pe.transpose(bank[4 + k // 2][:, c0:c0 + P], h[:, t, k * P:(k + 1) * P], ident)
                        if t == TT - 1 and k % 2 == 1:
                            ins.then_inc(tr_done, 1)

            def await_hT(stage):
                pe.wait_ge(hT_by_act, 2 * stage + 2)
                pe.wait_ge(hT_by_dve, 2 * stage + 2)

            def project(n0, c, banks):
                for j in range(2):
                    await_tile(pe, n0 + 2 * c + j)
                s0 = (n0 + 2 * c) % RING_SLOTS
                for t in range(TT):
                    for k in range(KD):
                        ins = pe.matmul(banks[t][:, :], hT[:, k, t * P:(t + 1) * P],
                                        ring[:, s0:s0 + 2, k * GROUP:(k + 1) * GROUP],
                                        start=(k == 0), stop=(k == KD - 1))
                ins.then_inc(tile_used, 2)

            def mixer(layer):
                n0 = MIX0[layer]
                transpose_tokens(3 * layer, h_ready, 4 * layer)
                await_hT(3 * layer)
                pe.wait_ge(wf_in, 32 * (layer + 1))
                for k in range(KD):
                    ins = pe.matmul(bank[4][0:H_FOX, 0:S], wf[:, k, :], hT[:, k, :], start=(k == 0), stop=(k == KD - 1))
                ins.then_inc(forget_done, 1)
                for c in range(6):
                    if c >= 2:
                        pe.wait_ge(proj_copied, 12 * layer + 2 * c - 2)
                    project(n0, c, [bank[2 * (c % 2) + t] for t in range(TT)])
                    if c == 3:
                        pe.wait_ge(c_ready, layer + 1)
                        for t in range(TT):
                            pe.transpose(bank[4][:, t * H_FOX:(t + 1) * H_FOX], fox[:, 0, t * P:(t + 1) * P],
                                         ident[0:H_FOX, 0:H_FOX])
                        for hh in range(H_FOX):
                            ins = pe.matmul(bank[5 + hh // 2][:, (hh % 2) * S:(hh % 2 + 1) * S],
                                            const[0:H_FOX, C_SEL + hh * P:C_SEL + (hh + 1) * P], fox[:, 1, :],
                                            start=True, stop=True)
                        ins.then_inc(bias_done, 1)
                pe.wait_ge(rope_ready, 2 * layer + 2)
                pe.wait_ge(bias_ready, layer + 1)
                for f in range(8):
                    if f >= 4:
                        done = qkT_by_act if f % 2 == 0 else qkT_by_dve
                        pe.wait_ge(done, 4 * layer + (f - 4) // 2 + 1)
                    for cc in range(2):
                        for t in range(TT):
                            ins = pe.transpose(bank[4 + f % 4][:, cc * S + t * P:cc * S + (t + 1) * P],
                                               qkv[:, t, (2 * f + cc) * P:(2 * f + cc + 1) * P], ident)
                    ins.then_inc(qk_tr_done, 1)
                pe.wait_ge(qkT_by_act, 4 * layer + 4)
                pe.wait_ge(qkT_by_dve, 4 * layer + 4)
                pe.wait_ge(proj_copied, 12 * layer + 12)

                def scores(hh):
                    if hh >= 2:
                        pe.wait_ge(logits_ready, NH * layer + hh - 1)
                    c, b = hh // 2, HD * (hh % 2)
                    q, k = qkT[b:b + HD, c, :], qkT[b:b + HD, KD + c, :]
                    pe.matmul(bank[hh % 2][:, 0:P], q[:, 0:P], k[:, 0:P], start=True, stop=True)
                    pe.matmul(bank[hh % 2][:, P:TRI], q[:, P:S], k, start=True, stop=True).then_inc(scores_done, 1)

                scores(0)
                scores(1)
                for hh in range(NH):
                    if hh < H_FOX + H_MOBA:
                        pe.wait_ge(exp_done, NH * layer + hh + 1)
                    else:
                        pe.wait_ge(weighted, (NH - H_FOX - H_MOBA) * layer + hh - H_FOX - H_MOBA + 1)
                    if hh >= 2:
                        pe.wait_ge(probsT_ready, NH * layer + hh - 1)
                    for blk in range(3):
                        ins = pe.transpose(bank[2 + hh % 2][:, blk * P:(blk + 1) * P],
                                           probs[:, hh % 2, blk * P:(blk + 1) * P], ident)
                    ins.then_inc(probs_tr_done, 1)
                    if hh + 2 < NH:
                        scores(hh + 2)
                    q4 = hh // 4
                    if hh % 4 == 0 and q4 >= 2:
                        pe.wait_ge(o_ready, 4 * layer + q4 - 1)
                    pe.wait_ge(probsT_ready, NH * layer + hh + 1)
                    pT = probsT[:, hh % 2, :]
                    v = [qkv[:, t, 2 * D + hh * HD:2 * D + (hh + 1) * HD] for t in range(TT)]
                    c0 = (hh % 4) * HD
                    pe.matmul(bank[4 + q4 % 2][:, c0:c0 + HD], pT[:, 0:P], v[0], start=True, stop=True)
                    pe.matmul(bank[4 + q4 % 2][:, S + c0:S + c0 + HD], pT[:, P:2 * P], v[0], start=True, stop=False)
                    pe.matmul(bank[4 + q4 % 2][:, S + c0:S + c0 + HD], pT[:, 2 * P:TRI], v[1], start=False, stop=True
                              ).then_inc(pv_done, 1)
                transpose_tokens(3 * layer + 1, y_ready, 2 * layer)
                await_hT(3 * layer + 1)
                for half in range(2):
                    project(n0 + 12, half, [bank[2 * half + t] for t in range(TT)])

            def up(G, g, n0, width, moving, trip=0):
                n = n0 + up_tile(g)
                for j in range(2):
                    await_tile(pe, n + j, trip)
                if G >= 2:
                    pe.wait_ge(hid_done, G - 1 + trip * NG)

                def products(cols):
                    for j in range(2):
                        w = slot(n + j).rearrange("p (k c) -> p k c", k=KD)
                        for c in range(CH):
                            for k in range(KD):
                                ins = pe.matmul(bank[2 * j + g % 2][:, c * width:c * width + cols],
                                                w[:, k, c * P:(c + 1) * P], moving(k, cols),
                                                start=(k == 0), stop=(k == KD - 1))
                        ins.then_inc(tile_used, 1)
                return products

            def down(g, n0, rows, banks, trip=0, G=0):
                n = n0 + down_tile(g)
                await_tile(pe, n, trip)
                pe.wait_ge(hid_done, G + 1 + trip * NG)
                w = slot(n).rearrange("p (c n) -> p c n", c=CH)
                for c in range(CH):
                    for t in range(len(banks) // 2):
                        for half in range(2):
                            ins = pe.matmul(banks[2 * t + half][0:rows, :],
                                            hid[:, g % 2, c * S + t * P:c * S + (t + 1) * P] if len(banks) == 4
                                            else hid[:, g % 2, c * CAP:c * CAP + rows],
                                            w[:, c, half * 512:(half + 1) * 512],
                                            start=(g == 0 and c == 0), stop=(g == NG - 1 and c == CH - 1))
                ins.then_inc(tile_used, 1)

            pe.wait_ge(const_in, 16)
            mixer(0)
            transpose_tokens(2, h_ready, 2)
            await_hT(2)
            for g in range(NG + 1):
                if g < NG:
                    up(g, g, FFN0[0], S, lambda k, cols: hT[:, k, :])(S)
                if g:
                    down(g - 1, FFN0[0], P, bank[4:8], G=g - 1)
            mixer(1)
            transpose_tokens(5, h_ready, 6)
            await_hT(5)
            pe.wait_ge(small_in, 16)
            for t in range(TT):
                for k in range(KD):
                    ins = pe.matmul(bank[4][:, t * NE:(t + 1) * NE], hT[:, k, t * P:(t + 1) * P], wr[:, k, :],
                                    start=(k == 0), stop=(k == KD - 1))
            ins.then_inc(router_done, 1)
            pe.wait_ge(mask_ready, 1)
            pe.matmul(bank[5][:, 0:NE], before, mask[:, 0, :], start=True, stop=True)
            pe.matmul(bank[5][:, NE:2 * NE], ones, mask[:, 0, :], start=True, stop=False)
            pe.matmul(bank[5][:, NE:2 * NE], before, mask[:, 1, :], start=False, stop=True)
            pe.matmul(bank[6][0:1, 0:NE], ones[:, 0:1], mask[:, 0, :], start=True, stop=False)
            pe.matmul(bank[6][0:1, 0:NE], ones[:, 0:1], mask[:, 1, :], start=False, stop=True).then_inc(pos_done, 1)

            def gather(e):
                for half in range(2):
                    for k in range(4):
                        for t in range(TT):
                            rows = (pick[:, 0, t, :] if isinstance(e, int)
                                    else pick[:, bass.ds(e, 1), t, :].rearrange("p e c -> p (e c)"))
                            kk = half * 4 + k
                            ins = pe.matmul(bank[6 + half][:, k * CAP:(k + 1) * CAP], h[:, t, kk * P:(kk + 1) * P],
                                            rows, start=(t == 0), stop=(t == TT - 1))
                    ins.then_inc(gather_done, 1)

            def scatter(i, trip):
                pe.wait_ge(spread_ready, i + 1)
                pe.wait_ge(y_copied, trip * 2 + 2)
                for item in range(4):
                    t, half = item // 2, item % 2
                    if item >= 2:
                        pe.wait_ge(scatter_added, 4 * i + item - 1)
                    pe.matmul(bank[6 + half][:, :], spread[:, t * P:(t + 1) * P], y_sb[:, half * 512:(half + 1) * 512],
                              start=True, stop=True).then_inc(scatter_done, 1)

            def experts(pass_no):
                pe.wait_ge(pick_ready, pass_no + 1)
                gather(0)
                with pe.Fori(0, NE) as e:
                    trip = moe_trip(pass_no, e)
                    i = e + (NE + 1) * pass_no
                    n_tok = pe.value_load(counts[0:1, bass.ds(e, 1)], min_val=0, max_val=S)
                    pe.wait_ge(hg_ready, 2 * i + 2)
                    parity = e % 2

                    def moving(k, cols):
                        return hg[:, bass.ds(parity, 1), k, 0:cols].rearrange("p b c -> p (b c)")

                    for g in range(NG + 1):
                        if g < NG:
                            products = up(NG + g, g, FFN0[1], CAP, moving, trip)
                            if pass_no == 0:
                                with pe.If(n_tok > NARROW[1]):
                                    products(CAP)
                                with pe.Else():
                                    with pe.If(n_tok > NARROW[0]):
                                        products(NARROW[1])
                                    with pe.Else():
                                        products(NARROW[0])
                                    pe.nop()
                            else:
                                products(CAP)
                        if g == 0:
                            scatter(i, trip)
                        else:
                            down(g - 1, FFN0[1], P, bank[4:6], trip, NG + g - 1)
                        if g == 5:
                            pe.wait_ge(gated_ready, 2 * trip + 2)
                            pe.wait_ge(scatter_added, 4 * i + 4)
                            for t in range(TT):
                                ins = pe.transpose(bank[6][:, t * P:(t + 1) * P], gated[:, t, :], ident)
                            ins.then_inc(spread_done, 1)
                        if g == 8:
                            pe.wait_ge(spread_ready, i + 2)
                            gather(e + 1)
                pe.wait_ge(hg_ready, 2 * (NE + 1) * (pass_no + 1))
                scatter((NE + 1) * pass_no + NE, NE * (pass_no + 1))

            pe.wait_ge(counts_ready, 1)
            experts(0)
            most = pe.value_load(counts[0:1, NE:NE + 1], min_val=0, max_val=S)
            with pe.If(most > CAP):
                experts(1)
                pe.nop()


NAMES = ["x"] + [f"l{l}_{n}" for l in range(2) for n in ("norm_mix", "w_in", "b_f", "mix_gain", "w_out", "norm_ffn")] + [
    "l0_w1", "l0_w3", "l0_w2", "l1_w_router", "l1_we1", "l1_we3", "l1_we2", "final_norm"]


def constants():
    import numpy as np
    c = np.zeros((P, C_END), np.float32)
    r = np.arange(P)
    c[:, C_ID:C_ID + P] = np.eye(P)
    c[:, C_LT:C_LT + P] = r[:, None] < r[None, :]
    c[:, C_ONE:C_ONE + P] = 1.0
    c[:, C_IOTA:C_IOTA + P] = r[None, :]
    for j, (q0, k0) in enumerate(((0, 0), (P, 0), (P, P))):
        dist = (q0 + r[:, None]) - (k0 + r[None, :])
        causal = dist >= 0
        times = sum(((dist % dil == 0) & causal & (dist <= win // dil * dil)).astype(int)
                    for win, dil in ((128, 1), (512, 4), (2048, 16)))
        sl = slice(j * P, (j + 1) * P)
        c[:, C_CAUSAL:C_CAUSAL + TRI][:, sl] = np.where(causal, 0.0, -1e30)
        c[:, C_UNION:C_UNION + TRI][:, sl] = np.where(times > 0, 0.0, -1e30)
        c[:, C_MULT:C_MULT + TRI][:, sl] = times
    inv = np.float32(500000.0) ** (-np.arange(0, ROT, 2, dtype=np.float32) / np.float32(ROT))
    ang = np.arange(S, dtype=np.float32)[:, None] * inv[None, :].astype(np.float32)
    for t in range(TT):
        c[:, C_COS + t * HALF:C_COS + (t + 1) * HALF] = np.cos(ang[t * P:(t + 1) * P])
        c[:, C_SIN + t * HALF:C_SIN + (t + 1) * HALF] = np.sin(ang[t * P:(t + 1) * P])
    for hh in range(H_FOX):
        c[hh, C_SEL + hh * P:C_SEL + (hh + 1) * P] = 1.0
    return c


def kernel(**inputs):
    import numpy as np
    import concourse.bacc as bacc
    from concourse.bass_utils import run_bass_kernel_spmd

    nc = bacc.Bacc("TRN2", target_bir_lowering=False, num_devices=1)
    arrays, args = {}, {}
    given = {name: np.ascontiguousarray(inputs[name]) for name in NAMES}
    given["const"] = constants()
    for name, v in given.items():
        arrays[f"in_{name}"] = v
        args[name] = nc.dram_tensor(f"in_{name}", v.shape, mybir.dt.from_np(v.dtype), kind="ExternalInput").ap()
    out = nc.dram_tensor("out", (1, S, D), F32, kind="ExternalOutput").ap()
    hybrid_trunk(nc, args, out)
    r = run_bass_kernel_spmd(nc, [arrays], core_ids=[0])
    return r.results[0]["out"]
```

```python
import concourse.bass as bass
from concourse import mybir
from contextlib import ExitStack

F32 = mybir.dt.float32
F32R = mybir.dt.float32r
I32 = mybir.dt.int32
U32 = mybir.dt.uint32
ALU = mybir.AluOpType
ACT = mybir.ActivationFunctionType
AX = mybir.AxisListType.X

P = 128
D = 1024
S = 256
HD = 64
NH = 16
H_FOX = 5
H_MOBA = 5
F = 3584
NE = 8
EPS = 1e-6
TT = S // P
KD = D // P
ROT = HD // 4
HALF = ROT // 2
WIDE = 512
GROUP = WIDE
CH = GROUP // P
NG = F // GROUP
RAW_SLOTS = 6
CUT_SLOTS = 7
KT = KD // 2
TILE = KT * WIDE
HALF_TILE = TILE // 2
CT = TILE // D
PER_FFN = 6 * NG
MIX_TILES = 16
CAP = P
SCATTER_BANKS = (1, 3, 4, 5)
SCATTER, SPREAD = 3, 21
TRI = 3 * P
GROUPS = ((0, H_FOX * HD), (H_FOX * HD, (H_FOX + H_MOBA) * HD), ((H_FOX + H_MOBA) * HD, D))

C_ID, C_LT, C_ONE, C_IOTA = 0, 128, 256, 384
C_CAUSAL, C_UNION, C_MULT = 512, 512 + TRI, 512 + 2 * TRI
C_COS = 512 + 3 * TRI
C_SIN = C_COS + TT * HALF
C_SEL = C_SIN + TT * HALF
C_END = C_SEL + H_FOX * P


def up_tile(g):
    return 0 if g == 0 else 6 * g - 2


def down_tile(g):
    return 6 * g + 8 if g < NG - 1 else PER_FFN - 2


def ffn_order():
    order = [None] * PER_FFN
    for g in range(NG):
        for half in range(2):
            order[up_tile(g) + half] = ("w1", g, half)
            order[up_tile(g) + 2 + half] = ("w3", g, half)
            order[down_tile(g) + half] = ("w2", g, half)
    return order


def hybrid_trunk(nc, a, out):
    ctx = ExitStack()
    with ctx:
        def sb(name, shape, dt=F32):
            return ctx.enter_context(nc.sbuf_tensor(name, shape, dt))

        def sem(name):
            return ctx.enter_context(nc.semaphore(name))

        raw = sb("raw", [P, RAW_SLOTS, TILE])
        w_hi = sb("w_hi", [P, CUT_SLOTS, HALF_TILE], F32R)
        w_lo = sb("w_lo", [P, CUT_SLOTS, HALF_TILE], F32R)
        const = sb("const", [P, C_END])
        x = sb("x_res", [P, TT, D])
        h = sb("h_tok", [P, TT, D])
        hT_hi = sb("hT_hi", [P, KD, S], F32R)
        hT_lo = sb("hT_lo", [P, KD, S], F32R)
        gain = sb("gain", [P, D])
        work = sb("work", [P, TT * 3 * D + 2 * KD * S])
        hid = sb("hid", [P, TT, GROUP])
        hidT_hi = sb("hidT_hi", [P, TT, CH * P], F32R)
        hidT_lo = sb("hidT_lo", [P, TT, CH * P], F32R)
        probsT = sb("probsT", [P, 2, TRI])
        wf = sb("w_forget", [P, KD, H_FOX])
        bf = sb("b_forget", [H_FOX, 1])
        wr = sb("w_router", [P, KD, NE])
        wf_cut = sb("w_forget_cut", [P, KD, 2, H_FOX], F32R)
        wr_cut = sb("w_router_cut", [P, KD, 2, NE], F32R)
        small = sb("small", [P, 320])
        idx8 = sb("idx8", [P, TT, 8], U32)
        counts = sb("counts", [1, 16], I32)

        ident = const[:, C_ID:C_ID + P]
        before = const[:, C_LT:C_LT + P]
        ones = const[:, C_ONE:C_ONE + P]
        iota = const[:, C_IOTA:C_IOTA + P]
        qkv = work[:, 0:TT * 3 * D].rearrange("p (t n) -> p t n", t=TT)
        qkT = work[:, TT * 3 * D:].rearrange("p (c t) -> p c t", c=2 * KD)
        o_tok = qkv[:, :, 0:D]
        fox_bias = h[:, :, :].rearrange("p t d -> p (t d)")[:, 0:H_FOX * TRI].rearrange("p (h n) -> p h n", h=H_FOX)
        probs = hid[:, :, 0:TRI]
        o = 0
        pick = work[:, o:o + NE * TT * CAP].rearrange("p (e t c) -> p e t c", e=NE, t=TT)
        o += NE * TT * CAP
        gated = work[:, o:o + TT * CAP].rearrange("p (t c) -> p t c", t=TT)
        o += TT * CAP
        spread = work[:, o:o + S]
        o += S
        y_sb = work[:, o:o + D]
        hg_hi = hT_hi[:, :, 0:CAP]
        hg_lo = hT_lo[:, :, 0:CAP]
        ss = small[:, 0:8]
        rstd = small[:, 8:16]
        newton = small[:, 306:314]
        negmax = small[:, 16:48].rearrange("p (h t) -> p h t", t=TT)
        rowmax = small[:, 48:80].rearrange("p (h t) -> p h t", t=TT)
        rowsum = small[:, 80:112].rearrange("p (t h) -> p t h", t=TT)
        rinv = small[:, 112:144].rearrange("p (t h) -> p t h", t=TT)
        cT = small[:, 144:144 + TT * H_FOX].rearrange("p (t h) -> p t h", t=TT)
        lg = small[:, 160:176].rearrange("p (t e) -> p t e", t=TT)
        top = small[:, 176:192].rearrange("p (t e) -> p t e", t=TT)
        idf = small[:, 192:208].rearrange("p (t e) -> p t e", t=TT)
        pick0 = small[:, 208:224].rearrange("p (t e) -> p t e", t=TT)
        pick1 = small[:, 224:240].rearrange("p (t e) -> p t e", t=TT)
        mask = small[:, 240:256].rearrange("p (t e) -> p t e", t=TT)
        gate = small[:, 256:272].rearrange("p (t e) -> p t e", t=TT)
        pos = small[:, 272:288].rearrange("p (t e) -> p t e", t=TT)
        dz = small[:, 288:290]
        z = small[:, 290:292]
        den = small[:, 292:294]
        g0 = small[:, 294:296]
        g1 = small[:, 296:298]
        cnt_f = small[0:1, 298:306]
        early = probsT[:, :, :].rearrange("p b n -> p (b n)")
        fox = early[0:H_FOX, 0:2 * S].rearrange("h (r t) -> h r t", r=2)
        rope_t = early[:, 2 * S:2 * S + 2 * (NH - H_FOX) * HALF]

        bank = [ctx.enter_context(nc.psum_tensor(f"bank{i}", [P, 512], F32)) for i in range(8)]

        const_in, x_in, small_in = sem("const_in"), sem("x_in"), sem("small_in")
        wf_in = sem("wf_in")
        gain_in = sem("gain_in")
        tile_in = [sem(f"tile_in{i}") for i in range(RAW_SLOTS)]
        hi_done, cut_done, half_used = sem("hi_done"), sem("cut_done"), sem("half_used")
        h_ready = sem("h_ready")
        y_ready = sem("y_ready")
        var_ready, root_ready = sem("var_ready"), sem("root_ready")
        tr_done = sem("tr_done")
        hT_hi_done, hT_done = sem("hT_hi_done"), sem("hT_done")
        wf_hi_done, wf_cut_done, wr_hi_done, wr_cut_done = (sem("wf_hi_done"), sem("wf_cut_done"),
                                                            sem("wr_hi_done"), sem("wr_cut_done"))
        forget_done, forget_ln, c_ready = sem("forget_done"), sem("forget_ln"), sem("c_ready")
        proj_copied = sem("proj_copied")
        bias_done, bias_ready = sem("bias_done"), sem("bias_ready")
        rope_ready = sem("rope_ready")
        qk_tr_done, qkT_by_act, qkT_by_dve = sem("qk_tr_done"), sem("qkT_by_act"), sem("qkT_by_dve")
        scores_done, logits_ready, exp_done, weighted = (sem("scores_done"), sem("logits_ready"),
                                                         sem("exp_done"), sem("weighted"))
        probs_tr_done, probsT_ready, pv_done, o_ready = (sem("probs_tr_done"), sem("probsT_ready"),
                                                         sem("pv_done"), sem("o_ready"))
        silu_done, hid_done = sem("silu_done"), sem("hid_done")
        hid_tr_done, hidT_hi_done, hidT_done = sem("hid_tr_done"), sem("hidT_hi_done"), sem("hidT_done")
        router_done, top_ready, z_ready, mask_ready = (sem("router_done"), sem("top_ready"),
                                                       sem("z_ready"), sem("mask_ready"))
        pos_done, counts_ready = sem("pos_done"), sem("counts_ready")
        pick_ready = sem("pick_ready")
        gather_done, hg_hi_done, hg_ready = sem("gather_done"), sem("hg_hi_done"), sem("hg_ready")
        scatter_done, scatter_added = sem("scatter_done"), sem("scatter_added")
        gated_ready, spread_done, spread_ready = sem("gated_ready"), sem("spread_done"), sem("spread_ready")
        y_copied = sem("y_copied")
        out_ready, out_stored = sem("out_ready"), sem("out_stored")
        act_chain = sem("act_chain")
        dve_chain, dve_chain_pass, dve_chain_end = sem("dve_chain"), sem("dve_chain_pass"), sem("dve_chain_end")

        def linker(eng, s):
            n = [0]

            def link(ins):
                n[0] += 1
                ins.then_inc(s, 1)
                eng.wait_ge(s, n[0])
            return link

        MIX0 = (0, MIX_TILES + PER_FFN)
        FFN0 = (MIX_TILES, 2 * MIX_TILES + PER_FFN)

        silu_before_cut = {2 * (up_tile(g) + 2) + CUT_SLOTS - 1: g for g in range(NG)}
        mult_before_cut = {2 * (up_tile(g) + 4) + CUT_SLOTS - 1: g for g in range(NG)}
        hid_before_cut = {2 * (up_tile(g + 1) + 1 if g + 1 < NG else down_tile(g)) + CUT_SLOTS: g for g in range(NG)}

        def per_trip(trip, step):
            return 0 if isinstance(trip, int) and trip == 0 else trip * step

        def halves(n):
            return (2 * n, 2 * n + 1)

        def raw_half(m):
            n = m // 2
            return raw[:, n % RAW_SLOTS, (m % 2) * HALF_TILE:(m % 2 + 1) * HALF_TILE]

        def cut_hi(act, m, trip=0):
            n = m // 2
            act.wait_ge(tile_in[n % RAW_SLOTS], 16 * (n // RAW_SLOTS + 1) + per_trip(trip, 16 * (PER_FFN // RAW_SLOTS)))
            if m >= CUT_SLOTS:
                act.wait_ge(half_used, m - CUT_SLOTS + 1 + per_trip(trip, 2 * PER_FFN))
            act.copy(w_hi[:, m % CUT_SLOTS, :], raw_half(m)).then_inc(hi_done, 1)

        def cut_lo(dve, m, trip=0):
            dve.wait_ge(hi_done, m + 1 + per_trip(trip, 2 * PER_FFN))
            dve.tensor_tensor(w_lo[:, m % CUT_SLOTS, :], raw_half(m), w_hi[:, m % CUT_SLOTS, :].bitcast(F32),
                              ALU.subtract).then_inc(cut_done, 1)

        def moe_trip(pass_no, e):
            return e + NE * pass_no

        block = ctx.enter_context(nc.Block())

        @block.sync
        def _(sp):
            def load(n, src, trip=0):
                if n >= RAW_SLOTS:
                    sp.wait_ge(cut_done, 2 * (n - RAW_SLOTS + 1) + per_trip(trip, 2 * PER_FFN))
                shaped = raw[:, n % RAW_SLOTS, :].rearrange("p (k c) -> p k c", k=src.shape[1])
                sp.dma_start(shaped, src).then_inc(tile_in[n % RAW_SLOTS], 16)

            def d_tile(w, c, half):
                return w[half * D // 2:(half + 1) * D // 2, c * WIDE:(c + 1) * WIDE].rearrange("(k p) n -> p k n", p=P)

            def swiglu_src(kind, g, half, w1, w3, w2):
                if kind == "w2":
                    r0 = (2 * g + half) * CT * P
                    return w2[r0:r0 + CT * P, :].rearrange("(c p) n -> p c n", p=P)
                return d_tile(w1 if kind == "w1" else w3, g, half)

            sp.dma_start(x[:, :, :], a["x"].rearrange("b (t p) d -> p (b t) d", p=P)).then_inc(x_in, 16)
            sp.dma_start(const[:, :], a["const"]).then_inc(const_in, 16)
            sp.dma_start(wf[:, :, :], a["l0_w_in"][:, 3 * D:].rearrange("(k p) n -> p k n", p=P)).then_inc(wf_in, 16)
            sp.dma_start(bf[:, :], a["l0_b_f"].rearrange("(h o) -> h o", o=1)).then_inc(wf_in, 16)
            sp.dma_start(wr[:, :, :], a["l1_w_router"].rearrange("(k p) n -> p k n", p=P)).then_inc(small_in, 16)
            for layer in range(2):
                n = MIX0[layer]
                for name, width in (("w_in", 3 * D), ("w_out", D)):
                    w = a[f"l{layer}_{name}"]
                    for c in range(width // WIDE):
                        for half in range(2):
                            load(n, d_tile(w, c, half))
                            n += 1
                if layer == 0:
                    sp.wait_ge(c_ready, 1)
                    sp.dma_start(wf[:, :, :], a["l1_w_in"][:, 3 * D:].rearrange("(k p) n -> p k n", p=P)
                                 ).then_inc(wf_in, 16)
                    sp.dma_start(bf[:, :], a["l1_b_f"].rearrange("(h o) -> h o", o=1)).then_inc(wf_in, 16)
                if layer == 0:
                    for j, (kind, g, half) in enumerate(ffn_order()):
                        load(FFN0[0] + j, swiglu_src(kind, g, half, a["l0_w1"], a["l0_w3"], a["l0_w2"]))

            def experts(pass_no):
                with sp.Fori(0, NE) as e:
                    ws = [a[k][bass.ds(e, 1), :, :].rearrange("e r c -> (e r) c") for k in ("l1_we1", "l1_we3", "l1_we2")]
                    for j, (kind, g, half) in enumerate(ffn_order()):
                        load(FFN0[1] + j, swiglu_src(kind, g, half, *ws), moe_trip(pass_no, e))

            experts(0)
            sp.wait_ge(counts_ready, 1)
            most = sp.value_load(counts[0:1, NE:NE + 1], min_val=0, max_val=S)
            with sp.If(most > CAP):
                experts(1)
                sp.nop()
            for t in range(TT):
                sp.wait_ge(out_ready, t + 1)
                sp.dma_start(out[0, t * P:(t + 1) * P, :], h[:, t, :]).then_inc(out_stored, 16)
            sp.wait_ge(out_stored, 16 * TT)

        @block.gpsimd
        def _(pool):
            order = ("l0_norm_mix", "l0_mix_gain", "l0_norm_ffn", "l1_norm_mix", "l1_mix_gain", "l1_norm_ffn",
                     "final_norm")
            freed = ((h_ready, 2), (y_ready, 2), (h_ready, 4), (h_ready, 6), (y_ready, 4), (h_ready, 8))
            for i, name in enumerate(order):
                if i:
                    pool.wait_ge(*freed[i - 1])
                pool.dma_start(gain[:, :], a[name].partition_broadcast(P)).then_inc(gain_in, 16)

        @block.scalar
        def _(act):
            link = linker(act, act_chain)

            def copy_transposed(stage):
                for b in range(4):
                    act.wait_ge(tr_done, 4 * stage + b + 1)
                    act.copy(hT_hi[:, 2 * b:2 * b + 2, :], bank[4 + b][:, :].rearrange("p (k t) -> p k t", k=2)
                             ).then_inc(hT_hi_done, 1)

            def root(norm_no, n):
                act.wait_ge(var_ready, norm_no + 1)
                link(act.activation(rstd[:, 0:n], ss[:, 0:n], ACT.Ln))
                act.activation(rstd[:, 0:n], rstd[:, 0:n], ACT.Exp, scale=-0.5).then_inc(root_ready, 1)

            def mixer(layer):
                n0 = MIX0[layer]
                act.wait_ge(wf_in, 32 * (layer + 1))
                act.copy(wf_cut[:, :, 0, :], wf[:, :, :]).then_inc(wf_hi_done, 1)
                root(3 * layer, TT)
                if not layer:
                    for m in halves(0):
                        cut_hi(act, m)
                copy_transposed(3 * layer)
                if not layer:
                    for m in halves(1):
                        cut_hi(act, m)
                    act.wait_ge(small_in, 16)
                    act.copy(wr_cut[:, :, 0, :], wr[:, :, :]).then_inc(wr_hi_done, 1)
                for m in halves(n0 + 2):
                    cut_hi(act, m)
                act.wait_ge(forget_done, layer + 1)
                link(act.activation(fox[:, 0, :], bank[4][0:H_FOX, 0:S], ACT.Identity, bias=bf[:, :]))
                link(act.activation(fox[:, 1, :], fox[:, 0, :], ACT.Abs))
                link(act.activation(fox[:, 1, :], fox[:, 1, :], ACT.Exp, scale=-1.0))
                act.activation(fox[:, 1, :], fox[:, 1, :], ACT.Ln, bias=1.0).then_inc(forget_ln, 1)
                for c in range(6):
                    for m in halves(n0 + 2 * c + 3):
                        cut_hi(act, m)
                    act.wait_ge(half_used, 2 * (n0 + 2 * c + 2))
                    for t in range(TT):
                        act.activation(qkv[:, t, c * 512:(c + 1) * 512], bank[2 * (c % 2) + t][:, :], ACT.Copy,
                                       scale=(HD ** -0.5 if c < 2 else 1.0)).then_inc(proj_copied, 1)
                    for m in halves(n0 + 2 * c + 4):
                        cut_hi(act, m)
                for f in range(0, 8, 2):
                    act.wait_ge(qk_tr_done, 8 * layer + f + 1)
                    act.copy(qkT[:, 2 * f:2 * f + 2, :], bank[4 + f % 4][:, :].rearrange("p (c t) -> p c t", c=2)
                             ).then_inc(qkT_by_act, 1)

                def exps(hh):
                    act.wait_ge(logits_ready, NH * layer + hh + 1)
                    for t in range(TT):
                        lo, hi = (0, P) if t == 0 else (P, TRI)
                        row = probs[:, hh % 2, lo:hi]
                        ins = act.activation(row, row, ACT.Exp, bias=negmax[:, hh, t:t + 1],
                                             accum_out=rowsum[:, t, hh:hh + 1])
                    ins.then_inc(exp_done, 1)

                exps(0)
                for hh in range(NH):
                    if hh + 1 < NH:
                        exps(hh + 1)
                    act.wait_ge(probs_tr_done, NH * layer + hh + 1)
                    if hh >= 2:
                        act.wait_ge(pv_done, NH * layer + hh - 1)
                    act.copy(probsT[:, hh % 2, :], bank[2 + hh % 2][:, 0:TRI]).then_inc(probsT_ready, 1)
                root(3 * layer + 1, 3 * TT)
                copy_transposed(3 * layer + 1)
                for m in halves(n0 + 15) + halves(FFN0[layer]) + halves(FFN0[layer] + 1):
                    cut_hi(act, m)

            def silu(g, trip, tokens):
                n = FFN0[0 if tokens == TT else 1]
                act.wait_ge(half_used, 2 * (n + up_tile(g) + 2) + per_trip(trip, 2 * PER_FFN))
                for t in range(tokens):
                    act.activation(hid[:, t, :], bank[t][:, :], ACT.Silu).then_inc(silu_done, 1)

            def hid_hi(count, trip, tokens):
                for t in range(tokens):
                    act.wait_ge(hid_tr_done, count + t + 1 + per_trip(trip, NG))
                    act.copy(hidT_hi[:, t, :], bank[2 + t][:, :]).then_inc(hidT_hi_done, 1)

            mixer(0)
            n0 = FFN0[0]
            root(2, TT)
            copy_transposed(2)
            for m in range(4, 2 * PER_FFN + 4):
                if m in hid_before_cut:
                    hid_hi(TT * hid_before_cut[m], 0, TT)
                if m in silu_before_cut:
                    silu(silu_before_cut[m], 0, TT)
                cut_hi(act, 2 * n0 + m)
            mixer(1)
            root(5, TT)
            copy_transposed(5)
            for m in range(4, CUT_SLOTS):
                cut_hi(act, 2 * FFN0[1] + m)
            act.wait_ge(top_ready, 1)
            act.activation(z, dz, ACT.Exp).then_inc(z_ready, 1)

            def gathered_hi(trip):
                for half in range(2):
                    act.wait_ge(gather_done, per_trip(trip, 2) + half + 1)
                    act.copy(hg_hi[:, half * 4:half * 4 + 4, :], bank[4 + half][:, :].rearrange("p (k c) -> p k c", k=4)
                             ).then_inc(hg_hi_done, 1)

            def expert(pass_no, e, last):
                trip = moe_trip(pass_no, e)
                for m in range(CUT_SLOTS, 2 * PER_FFN + CUT_SLOTS):
                    if m in hid_before_cut:
                        hid_hi(TT * NG + hid_before_cut[m], trip, 1)
                        if hid_before_cut[m] == NG - 1 and not last:
                            gathered_hi(trip + 1)
                    if m in silu_before_cut:
                        silu(silu_before_cut[m], trip, 1)
                    if m < 2 * PER_FFN + CUT_SLOTS - 1 and not (last and m >= 2 * PER_FFN):
                        cut_hi(act, 2 * FFN0[1] + m, trip)
                act.wait_ge(half_used, 2 * (FFN0[1] + PER_FFN) + per_trip(trip, 2 * PER_FFN))
                for half in range(2):
                    act.copy(y_sb[:, half * 512:(half + 1) * 512], bank[6 + half][:, :]).then_inc(y_copied, 1)
                if not last:
                    cut_hi(act, 2 * (FFN0[1] + PER_FFN) + CUT_SLOTS - 1, trip)

            def experts(pass_no):
                if pass_no:
                    for m in range(CUT_SLOTS):
                        cut_hi(act, 2 * FFN0[1] + m, moe_trip(pass_no, 0))
                gathered_hi(moe_trip(pass_no, 0))
                with act.Fori(0, NE - 1) as e:
                    expert(pass_no, e, False)
                expert(pass_no, NE - 1, True)

            experts(0)
            act.wait_ge(counts_ready, 1)
            most = act.value_load(counts[0:1, NE:NE + 1], min_val=0, max_val=S)
            with act.If(most > CAP):
                experts(1)
                act.nop()
            root(6, TT)

        @block.vector
        def _(dve):
            link = linker(dve, dve_chain)

            def await_gain(i):
                dve.wait_ge(gain_in, 16 * (i + 1))
                return gain[:, :]

            def inverse_root(norm_no, n, link):
                dve.tensor_scalar(ss[:, 0:n], ss[:, 0:n], EPS, None, ALU.add).then_inc(var_ready, 1)
                dve.wait_ge(root_ready, norm_no + 1)
                link(dve.tensor_tensor(newton[:, 0:n], rstd[:, 0:n], rstd[:, 0:n], ALU.mult))
                link(dve.tensor_tensor(newton[:, 0:n], newton[:, 0:n], ss[:, 0:n], ALU.mult))
                link(dve.tensor_scalar(newton[:, 0:n], newton[:, 0:n], -0.5, 1.5, ALU.mult, ALU.add))
                link(dve.tensor_tensor(rstd[:, 0:n], rstd[:, 0:n], newton[:, 0:n], ALU.mult))

            def norm(gain_no, done, link):
                for t in range(TT):
                    link(dve.tensor_tensor_reduce(out=h[:, t, :], in0=x[:, t, :], in1=x[:, t, :], scale=1.0 / D, scalar=0.0,
                                                  op0=ALU.mult, op1=ALU.add, accum_out=ss[:, t:t + 1]))
                inverse_root(gain_no, TT, link)
                g = await_gain(gain_no)
                for t in range(TT):
                    dve.scalar_tensor_tensor(out=h[:, t, :], in0=x[:, t, :], scalar=rstd[:, t:t + 1], in1=g,
                                             op0=ALU.mult, op1=ALU.mult).then_inc(done, 1)

            def copy_transposed(stage):
                for b in range(4):
                    dve.wait_ge(hT_hi_done, 4 * stage + b + 1)
                    dve.tensor_tensor(hT_lo[:, 2 * b:2 * b + 2, :], bank[4 + b][:, :].rearrange("p (k t) -> p k t", k=2),
                                      hT_hi[:, 2 * b:2 * b + 2, :].bitcast(F32), ALU.subtract).then_inc(hT_done, 1)

            def mixer(layer):
                n0 = MIX0[layer]
                norm(3 * layer, h_ready, link)
                dve.wait_ge(wf_hi_done, layer + 1)
                dve.tensor_tensor(wf_cut[:, :, 1, :], wf[:, :, :], wf_cut[:, :, 0, :].bitcast(F32), ALU.subtract
                                  ).then_inc(wf_cut_done, 1)
                if not layer:
                    for m in halves(0):
                        cut_lo(dve, m)
                copy_transposed(3 * layer)
                if not layer:
                    for m in halves(1):
                        cut_lo(dve, m)
                    dve.wait_ge(wr_hi_done, 1)
                    dve.tensor_tensor(wr_cut[:, :, 1, :], wr[:, :, :], wr_cut[:, :, 0, :].bitcast(F32), ALU.subtract
                                      ).then_inc(wr_cut_done, 1)
                for m in halves(n0 + 2):
                    cut_lo(dve, m)
                dve.wait_ge(forget_ln, layer + 1)
                link(dve.tensor_scalar(fox[:, 0, :], fox[:, 0, :], 0.0, None, ALU.min))
                link(dve.tensor_tensor(fox[:, 1, :], fox[:, 0, :], fox[:, 1, :], ALU.subtract))
                link(dve.tensor_tensor_scan(fox[:, 0, :], ones[0:H_FOX, 0:1].to_broadcast([H_FOX, S]), fox[:, 1, :], 0.0, ALU.mult, ALU.add))
                dve.tensor_scalar(fox[:, 1, :], fox[:, 0, :], -1.0, None, ALU.mult).then_inc(c_ready, 1)
                for j in range(3, 11):
                    for m in halves(n0 + j):
                        cut_lo(dve, m)
                dve.wait_ge(bias_done, layer + 1)
                link(dve.tensor_copy(cT, bank[4][:, 0:TT * H_FOX].rearrange("p (t h) -> p t h", t=TT)))
                for hh in range(H_FOX):
                    src = bank[5 + hh // 2][:, (hh % 2) * S:(hh % 2 + 1) * S]
                    for t in range(TT):
                        lo, hi = (0, P) if t == 0 else (P, TRI)
                        link(dve.scalar_tensor_tensor(out=fox_bias[:, hh, lo:hi], in0=src[:, 0:hi - lo],
                                                      scalar=cT[:, t, hh:hh + 1],
                                                      in1=const[:, C_CAUSAL + lo:C_CAUSAL + hi],
                                                      op0=ALU.add, op1=ALU.add))
                dve.sem_inc(bias_ready, 1)
                for m in halves(n0 + 11):
                    cut_lo(dve, m)
                dve.wait_ge(proj_copied, 12 * layer + 8)
                for t in range(TT):
                    qk = qkv[:, t, 0:2 * D].rearrange("p (s h d) -> p s h d", s=2, h=NH)[:, :, H_FOX:, :]
                    n = NH - H_FOX
                    for s in range(2):
                        x1, x2 = qk[:, s, :, 0:HALF], qk[:, s, :, HALF:ROT]
                        cs = const[:, C_COS + t * HALF:C_COS + (t + 1) * HALF].unsqueeze(1).to_broadcast([P, n, HALF])
                        sn = const[:, C_SIN + t * HALF:C_SIN + (t + 1) * HALF].unsqueeze(1).to_broadcast([P, n, HALF])
                        ta = rope_t[:, 0:n * HALF].rearrange("p (h d) -> p h d", h=n)
                        tb = rope_t[:, n * HALF:2 * n * HALF].rearrange("p (h d) -> p h d", h=n)
                        link(dve.tensor_tensor(ta, x2, sn, ALU.mult))
                        link(dve.tensor_tensor(tb, x1, sn, ALU.mult))
                        link(dve.tensor_tensor(x1, x1, cs, ALU.mult))
                        link(dve.tensor_tensor(x2, x2, cs, ALU.mult))
                        link(dve.tensor_tensor(x1, x1, ta, ALU.subtract))
                        link(dve.tensor_tensor(x2, x2, tb, ALU.add))
                    dve.sem_inc(rope_ready, 1)
                for j in range(12, 15):
                    for m in halves(n0 + j):
                        cut_lo(dve, m)
                for f in range(1, 8, 2):
                    dve.wait_ge(qk_tr_done, 8 * layer + f + 1)
                    dve.tensor_copy(qkT[:, 2 * f:2 * f + 2, :], bank[4 + f % 4][:, :].rearrange("p (c t) -> p c t", c=2)
                                    ).then_inc(qkT_by_dve, 1)

                def logits(hh):
                    dve.wait_ge(scores_done, NH * layer + hh + 1)
                    if hh >= 2:
                        dve.wait_ge(probs_tr_done, NH * layer + hh - 1)
                    if hh < H_FOX:
                        bias = fox_bias[:, hh, :]
                    else:
                        c0 = C_CAUSAL if hh < H_FOX + H_MOBA else C_UNION
                        bias = const[:, c0:c0 + TRI]
                    for t in range(TT):
                        lo, hi = (0, P) if t == 0 else (P, TRI)
                        ins = dve.tensor_tensor_reduce(out=probs[:, hh % 2, lo:hi], in0=bank[hh % 2][:, lo:hi],
                                                       in1=bias[:, lo:hi], scale=1.0, scalar=-3.0e38, op0=ALU.add,
                                                       op1=ALU.max, accum_out=rowmax[:, hh, t:t + 1])
                        link(ins)
                    dve.tensor_scalar(negmax[:, hh, :], rowmax[:, hh, :], -1.0, None, ALU.mult
                                      ).then_inc(logits_ready, 1)

                logits(0)
                for hh in range(NH):
                    if hh + 1 < NH:
                        logits(hh + 1)
                    if hh >= H_FOX + H_MOBA:
                        dve.wait_ge(exp_done, NH * layer + hh + 1)
                        for t in range(TT):
                            lo, hi = (0, P) if t == 0 else (P, TRI)
                            row = probs[:, hh % 2, lo:hi]
                            ins = dve.tensor_tensor_reduce(out=row, in0=row, in1=const[:, C_MULT + lo:C_MULT + hi],
                                                           scale=1.0, scalar=0.0, op0=ALU.mult, op1=ALU.add,
                                                           accum_out=rowsum[:, t, hh:hh + 1])
                            if t == 0:
                                link(ins)
                        ins.then_inc(weighted, 1)
                    if hh % 4 == 3:
                        q4 = hh // 4
                        dve.wait_ge(pv_done, NH * layer + hh + 1)
                        link(dve.reciprocal(rinv[:, :, 4 * q4:4 * q4 + 4], rowsum[:, :, 4 * q4:4 * q4 + 4]))
                        src = bank[4 + q4 % 2][:, :].rearrange("p (t h d) -> p t h d", t=TT, h=4)
                        for t in range(TT):
                            link(dve.tensor_tensor(
                                o_tok[:, t, q4 * 4 * HD:(q4 + 1) * 4 * HD].rearrange("p (h d) -> p h d", h=4),
                                src[:, t, :, :],
                                rinv[:, t, 4 * q4:4 * q4 + 4].unsqueeze(2).to_broadcast([P, 4, HD]), ALU.mult))
                        dve.sem_inc(o_ready, 1)
                for t in range(TT):
                    for i, (lo, hi) in enumerate(GROUPS):
                        link(dve.tensor_tensor_reduce(out=h[:, t, lo:hi], in0=o_tok[:, t, lo:hi],
                                                      in1=o_tok[:, t, lo:hi], scale=1.0 / (hi - lo), scalar=0.0,
                                                      op0=ALU.mult, op1=ALU.add,
                                                      accum_out=ss[:, 3 * t + i:3 * t + i + 1]))
                inverse_root(3 * layer + 1, 6, link)
                gm = await_gain(3 * layer + 1)
                for t in range(TT):
                    for i, (lo, hi) in enumerate(GROUPS):
                        ins = dve.scalar_tensor_tensor(out=h[:, t, lo:hi], in0=o_tok[:, t, lo:hi],
                                                       scalar=rstd[:, 3 * t + i:3 * t + i + 1], in1=gm[:, lo:hi],
                                                       op0=ALU.mult, op1=ALU.mult)
                        if i < 2:
                            link(ins)
                    ins.then_inc(y_ready, 1)
                copy_transposed(3 * layer + 1)
                for m in halves(n0 + 15):
                    cut_lo(dve, m)
                for half in range(2):
                    dve.wait_ge(half_used, 2 * (n0 + 12 + 2 * half + 2))
                    for t in range(TT):
                        xs = x[:, t, half * 512:(half + 1) * 512]
                        link(dve.tensor_tensor(xs, xs, bank[2 * half + t][:, :], ALU.add))
                    if half == 0:
                        for m in halves(FFN0[layer]) + halves(FFN0[layer] + 1):
                            cut_lo(dve, m)

            def hidden(g, trip, tokens):
                n = FFN0[0 if tokens == TT else 1]
                count = TT * g if tokens == TT else TT * NG + g
                dve.wait_ge(half_used, 2 * (n + up_tile(g) + 4) + per_trip(trip, 2 * PER_FFN))
                for t in range(tokens):
                    dve.wait_ge(silu_done, count + t + 1 + per_trip(trip, NG))
                    dve.tensor_tensor(hid[:, t, :], hid[:, t, :], bank[2 + t][:, :], ALU.mult).then_inc(hid_done, 1)

            def hid_lo(count, trip, tokens):
                for t in range(tokens):
                    dve.wait_ge(hidT_hi_done, count + t + 1 + per_trip(trip, NG))
                    dve.tensor_tensor(hidT_lo[:, t, :], bank[2 + t][:, :], hidT_hi[:, t, :].bitcast(F32), ALU.subtract
                                      ).then_inc(hidT_done, 1)

            dve.wait_ge(x_in, 16)
            dve.wait_ge(const_in, 16)
            mixer(0)
            norm(2, h_ready, link)
            copy_transposed(2)
            for m in range(4, 2 * PER_FFN + 4):
                if m in hid_before_cut:
                    hid_lo(TT * hid_before_cut[m], 0, TT)
                if m in mult_before_cut:
                    hidden(mult_before_cut[m], 0, TT)
                cut_lo(dve, 2 * FFN0[0] + m)
            dve.wait_ge(half_used, 2 * (FFN0[0] + PER_FFN))
            for t in range(TT):
                for half in range(2):
                    xs = x[:, t, half * 512:(half + 1) * 512]
                    link(dve.tensor_tensor(xs, xs, bank[4 + 2 * t + half][:, :], ALU.add))
            mixer(1)
            norm(5, h_ready, link)
            copy_transposed(5)
            for m in range(4, CUT_SLOTS):
                cut_lo(dve, 2 * FFN0[1] + m)

            dve.wait_ge(router_done, 1)
            by_part = bank[4][:, 0:TT * 2 * NE].rearrange("p (t u e) -> p t u e", t=TT, u=2)
            link(dve.tensor_copy(lg, by_part[:, :, 0, :]))
            link(dve.tensor_tensor(lg, lg, by_part[:, :, 1, :], ALU.add))
            for t in range(TT):
                link(dve.max(top[:, t, :], lg[:, t, :]))
                link(dve.max_index(idx8[:, t, :], top[:, t, :], lg[:, t, :]))
            link(dve.tensor_copy(idf, idx8[:, :, :]))
            dve.tensor_tensor(dz, top[:, :, 1], top[:, :, 0], ALU.subtract).then_inc(top_ready, 1)
            for t in range(TT):
                link(dve.tensor_scalar(pick0[:, t, :], iota[:, 0:NE], idf[:, t, 0:1], None, ALU.is_equal))
                link(dve.tensor_scalar(pick1[:, t, :], iota[:, 0:NE], idf[:, t, 1:2], None, ALU.is_equal))
            dve.tensor_tensor(mask, pick0, pick1, ALU.add).then_inc(mask_ready, 1)
            dve.wait_ge(mask_ready, 1)
            dve.wait_ge(z_ready, 1)
            link(dve.tensor_scalar(den, z, 1.0, None, ALU.add))
            link(dve.reciprocal(g0, den))
            link(dve.tensor_tensor(g1, z, g0, ALU.mult))
            for t in range(TT):
                link(dve.tensor_scalar(gate[:, t, :], pick0[:, t, :], g0[:, t:t + 1], None, ALU.mult))
                link(dve.scalar_tensor_tensor(out=gate[:, t, :], in0=pick1[:, t, :], scalar=g1[:, t:t + 1],
                                              in1=gate[:, t, :], op0=ALU.mult, op1=ALU.add))
            dve.wait_ge(pos_done, 1)
            link(dve.scalar_tensor_tensor(out=pos, in0=bank[5][:, 0:TT * NE].rearrange("p (t e) -> p t e", t=TT),
                                          scalar=1.0, in1=mask, op0=ALU.add, op1=ALU.mult))
            link(dve.tensor_scalar(pos, pos, -1.0, None, ALU.add))
            link(dve.tensor_copy(counts[0:1, 0:NE], bank[6][0:1, 0:NE]))
            link(dve.tensor_reduce(cnt_f[0:1, 0:1], bank[6][0:1, 0:NE], AX, ALU.max))
            dve.tensor_copy(counts[0:1, NE:NE + 1], cnt_f[0:1, 0:1]).then_inc(counts_ready, 1)

            def experts(pass_no, link):
                if pass_no:
                    link(dve.tensor_scalar(pos, pos, float(-CAP), None, ALU.add))
                for t in range(TT):
                    dve.tensor_tensor(pick[:, :, t, :], iota.unsqueeze(1).to_broadcast([P, NE, CAP]),
                                      pos[:, t, :].unsqueeze(2).to_broadcast([P, NE, CAP]), ALU.is_equal
                                      ).then_inc(pick_ready, 1)
                dve.memset(spread, 0.0).then_inc(spread_ready, 1)
                for half in range(2):
                    dve.memset(y_sb[:, half * 512:(half + 1) * 512], 0.0).then_inc(y_copied, 1)
                if pass_no:
                    for m in range(CUT_SLOTS):
                        cut_lo(dve, 2 * FFN0[1] + m, moe_trip(pass_no, 0))

                def gathered_lo(trip):
                    for half in range(2):
                        dve.wait_ge(hg_hi_done, per_trip(trip, 2) + half + 1)
                        dve.tensor_tensor(hg_lo[:, half * 4:half * 4 + 4, :],
                                          bank[4 + half][:, :].rearrange("p (k c) -> p k c", k=4),
                                          hg_hi[:, half * 4:half * 4 + 4, :].bitcast(F32), ALU.subtract
                                          ).then_inc(hg_ready, 1)

                def add_scattered(i):
                    for item in range(4):
                        t, half = item // 2, item % 2
                        dve.wait_ge(scatter_done, 4 * i + item + 1)
                        xs = x[:, t, half * 512:(half + 1) * 512]
                        dve.tensor_tensor(xs, xs, bank[SCATTER_BANKS[item]][:, :], ALU.add).then_inc(scatter_added, 1)

                def expert(e, last):
                    trip = moe_trip(pass_no, e)
                    i = e + (NE + 1) * pass_no
                    for m in range(CUT_SLOTS, 2 * PER_FFN + CUT_SLOTS):
                        if m in hid_before_cut:
                            hid_lo(TT * NG + hid_before_cut[m], trip, 1)
                            if hid_before_cut[m] == NG - 1 and not last:
                                gathered_lo(trip + 1)
                        if m in mult_before_cut:
                            hidden(mult_before_cut[m], trip, 1)
                        if m == 2 * (SCATTER + 1) + CUT_SLOTS:
                            add_scattered(i)
                        if m == 2 * SPREAD - CUT_SLOTS:
                            for t in range(TT):
                                dve.tensor_scalar(
                                    gated[:, t, :], pick[:, bass.ds(e, 1), t, :].rearrange("p e c -> p (e c)"),
                                    gate[:, t, bass.ds(e, 1)], None, ALU.mult).then_inc(gated_ready, 1)
                        if m == 2 * (SPREAD + 1) + CUT_SLOTS:
                            dve.wait_ge(spread_done, trip + 1)
                            dve.tensor_copy(spread, bank[1][:, 0:S]).then_inc(spread_ready, 1)
                        if not (last and m >= 2 * PER_FFN):
                            cut_lo(dve, 2 * FFN0[1] + m, trip)

                gathered_lo(moe_trip(pass_no, 0))
                with dve.Fori(0, NE - 1) as e:
                    expert(e, False)
                expert(NE - 1, True)
                add_scattered((NE + 1) * pass_no + NE)

            experts(0, link)
            dve.wait_ge(scatter_added, 4 * (NE + 1))
            most = dve.value_load(counts[0:1, NE:NE + 1], min_val=0, max_val=S)
            with dve.If(most > CAP):
                experts(1, linker(dve, dve_chain_pass))
                dve.wait_ge(scatter_added, 8 * (NE + 1))
                dve.nop()
            norm(6, out_ready, linker(dve, dve_chain_end))

        @block.tensor
        def _(pe):
            def transpose_tokens(stage, ready, value):
                for t in range(TT):
                    pe.wait_ge(ready, value + t + 1)
                    for k in range(KD):
                        c0 = (k % 2) * S + t * P
                        ins = pe.transpose(bank[4 + k // 2][:, c0:c0 + P], h[:, t, k * P:(k + 1) * P], ident)
                        if t == TT - 1 and k % 2 == 1:
                            ins.then_inc(tr_done, 1)

            def await_hT(stage):
                pe.wait_ge(hT_done, 4 * stage + 4)

            def await_cut(m, trip=0):
                pe.wait_ge(cut_done, m + 1 + per_trip(trip, 2 * PER_FFN))

            def product(out, a_hi, a_lo, m, sl, first, last):
                hi, lo = w_hi[:, m % CUT_SLOTS, sl], w_lo[:, m % CUT_SLOTS, sl]
                pe.matmul(out, a_hi, hi, start=first, stop=False)
                pe.matmul(out, a_hi, lo, start=False, stop=False)
                return pe.matmul(out, a_lo, hi, start=False, stop=last)

            def d_product(n, half, a_hi, a_lo, banks, trip=0):
                for u, m in enumerate(halves(n)):
                    await_cut(m, trip)
                    for t in range(len(banks)):
                        for k in range(KT // 2):
                            kk = half * KT + u * (KT // 2) + k
                            ins = product(banks[t][:, :], a_hi[:, kk, t * P:(t + 1) * P],
                                          a_lo[:, kk, t * P:(t + 1) * P], m, slice(k * WIDE, (k + 1) * WIDE),
                                          kk == 0, kk == KD - 1)
                    ins.then_inc(half_used, 1)

            def project(n0, c, banks):
                for half in range(2):
                    d_product(n0 + 2 * c + half, half, hT_hi, hT_lo, banks)

            def mixer(layer):
                n0 = MIX0[layer]
                transpose_tokens(3 * layer, h_ready, 4 * layer)
                await_hT(3 * layer)
                pe.wait_ge(wf_cut_done, layer + 1)
                for k in range(KD):
                    for w_part, part in ((0, hT_hi), (1, hT_hi), (0, hT_lo)):
                        ins = pe.matmul(bank[4][0:H_FOX, 0:S], wf_cut[:, k, w_part, :], part[:, k, :],
                                        start=(k == 0 and w_part == 0 and part is hT_hi),
                                        stop=(k == KD - 1 and part is hT_lo))
                ins.then_inc(forget_done, 1)
                for c in range(6):
                    if c >= 2:
                        pe.wait_ge(proj_copied, 12 * layer + 2 * c - 2)
                    project(n0, c, [bank[2 * (c % 2) + t] for t in range(TT)])
                    if c == 3:
                        pe.wait_ge(c_ready, layer + 1)
                        for t in range(TT):
                            pe.transpose(bank[4][:, t * H_FOX:(t + 1) * H_FOX], fox[:, 0, t * P:(t + 1) * P],
                                         ident[0:H_FOX, 0:H_FOX])
                        for hh in range(H_FOX):
                            ins = pe.matmul(bank[5 + hh // 2][:, (hh % 2) * S:(hh % 2 + 1) * S],
                                            const[0:H_FOX, C_SEL + hh * P:C_SEL + (hh + 1) * P], fox[:, 1, :],
                                            start=True, stop=True)
                        ins.then_inc(bias_done, 1)
                pe.wait_ge(rope_ready, 2 * layer + 2)
                pe.wait_ge(bias_ready, layer + 1)
                for f in range(8):
                    if f >= 4:
                        done = qkT_by_act if f % 2 == 0 else qkT_by_dve
                        pe.wait_ge(done, 4 * layer + (f - 4) // 2 + 1)
                    for cc in range(2):
                        for t in range(TT):
                            ins = pe.transpose(bank[4 + f % 4][:, cc * S + t * P:cc * S + (t + 1) * P],
                                               qkv[:, t, (2 * f + cc) * P:(2 * f + cc + 1) * P], ident)
                    ins.then_inc(qk_tr_done, 1)
                pe.wait_ge(qkT_by_act, 4 * layer + 4)
                pe.wait_ge(qkT_by_dve, 4 * layer + 4)
                pe.wait_ge(proj_copied, 12 * layer + 12)

                def scores(hh):
                    if hh >= 2:
                        pe.wait_ge(logits_ready, NH * layer + hh - 1)
                    c, b = hh // 2, HD * (hh % 2)
                    q, k = qkT[b:b + HD, c, :], qkT[b:b + HD, KD + c, :]
                    pe.matmul(bank[hh % 2][:, 0:P], q[:, 0:P], k[:, 0:P], start=True, stop=True)
                    pe.matmul(bank[hh % 2][:, P:TRI], q[:, P:S], k, start=True, stop=True).then_inc(scores_done, 1)

                scores(0)
                scores(1)
                for hh in range(NH):
                    if hh < H_FOX + H_MOBA:
                        pe.wait_ge(exp_done, NH * layer + hh + 1)
                    else:
                        pe.wait_ge(weighted, (NH - H_FOX - H_MOBA) * layer + hh - H_FOX - H_MOBA + 1)
                    if hh >= 2:
                        pe.wait_ge(probsT_ready, NH * layer + hh - 1)
                    for blk in range(3):
                        ins = pe.transpose(bank[2 + hh % 2][:, blk * P:(blk + 1) * P],
                                           probs[:, hh % 2, blk * P:(blk + 1) * P], ident)
                    ins.then_inc(probs_tr_done, 1)
                    if hh + 2 < NH:
                        scores(hh + 2)
                    q4 = hh // 4
                    if hh % 4 == 0 and q4 >= 2:
                        pe.wait_ge(o_ready, 4 * layer + q4 - 1)
                    pe.wait_ge(probsT_ready, NH * layer + hh + 1)
                    pT = probsT[:, hh % 2, :]
                    v = [qkv[:, t, 2 * D + hh * HD:2 * D + (hh + 1) * HD] for t in range(TT)]
                    c0 = (hh % 4) * HD
                    pe.matmul(bank[4 + q4 % 2][:, c0:c0 + HD], pT[:, 0:P], v[0], start=True, stop=True)
                    pe.matmul(bank[4 + q4 % 2][:, S + c0:S + c0 + HD], pT[:, P:2 * P], v[0], start=True, stop=False)
                    pe.matmul(bank[4 + q4 % 2][:, S + c0:S + c0 + HD], pT[:, 2 * P:TRI], v[1], start=False, stop=True
                              ).then_inc(pv_done, 1)
                transpose_tokens(3 * layer + 1, y_ready, 2 * layer)
                await_hT(3 * layer + 1)
                for half in range(2):
                    project(n0 + 12, half, [bank[2 * half + t] for t in range(TT)])

            def swiglu(n0, trip, tokens, a_hi, a_lo, y_banks, behind):
                count = 0 if tokens == TT else TT * NG

                def transpose_hid(g):
                    for t in range(tokens):
                        pe.wait_ge(hid_done, count + tokens * g + t + 1 + per_trip(trip, NG))
                        for c in range(CH):
                            ins = pe.transpose(bank[2 + t][:, c * P:(c + 1) * P], hid[:, t, c * P:(c + 1) * P], ident)
                        ins.then_inc(hid_tr_done, 1)

                for j, (kind, g, half) in enumerate(ffn_order()):
                    n = n0 + j
                    if kind == "w1" and half == 0 and g:
                        pe.wait_ge(silu_done, count + tokens * g + per_trip(trip, NG))
                    if kind == "w3" and half == 0 and g:
                        pe.wait_ge(hidT_done, count + tokens * g + per_trip(trip, NG))
                    if kind == "w2":
                        if half == 0:
                            pe.wait_ge(hidT_done, count + tokens * (g + 1) + per_trip(trip, NG))
                        for c, m in enumerate(halves(n)):
                            await_cut(m, trip)
                            cc = CT * half + c
                            for t in range(tokens):
                                for out in range(2):
                                    ins = product(y_banks[2 * t + out][:, :], hidT_hi[:, t, cc * P:(cc + 1) * P],
                                                  hidT_lo[:, t, cc * P:(cc + 1) * P], m,
                                                  slice(out * WIDE, (out + 1) * WIDE),
                                                  g == 0 and cc == 0, g == NG - 1 and cc == CH - 1)
                            ins.then_inc(half_used, 1)
                    else:
                        b0 = 0 if kind == "w1" else 2
                        d_product(n, half, a_hi, a_lo, [bank[b0 + t] for t in range(tokens)], trip)
                    if kind == "w1" and half == 0 and g:
                        transpose_hid(g - 1)
                    if j == down_tile(NG - 2) + 1:
                        transpose_hid(NG - 1)
                    if j in behind:
                        behind[j]()

            pe.wait_ge(const_in, 16)
            mixer(0)
            transpose_tokens(2, h_ready, 2)
            await_hT(2)
            swiglu(FFN0[0], 0, TT, hT_hi, hT_lo, bank[4:8], {})
            mixer(1)
            transpose_tokens(5, h_ready, 6)
            await_hT(5)
            pe.wait_ge(wr_cut_done, 1)
            for t in range(TT):
                for k in range(KD):
                    for part in (hT_hi, hT_lo):
                        ins = pe.matmul(bank[4][:, t * 2 * NE:(t + 1) * 2 * NE], part[:, k, t * P:(t + 1) * P],
                                        wr_cut[:, k, :, :].rearrange("p u e -> p (u e)"),
                                        start=(k == 0 and part is hT_hi), stop=(k == KD - 1 and part is hT_lo))
            ins.then_inc(router_done, 1)
            pe.wait_ge(mask_ready, 1)
            pe.matmul(bank[5][:, 0:NE], before, mask[:, 0, :], start=True, stop=True)
            pe.matmul(bank[5][:, NE:2 * NE], ones, mask[:, 0, :], start=True, stop=False)
            pe.matmul(bank[5][:, NE:2 * NE], before, mask[:, 1, :], start=False, stop=True)
            pe.matmul(bank[6][0:1, 0:NE], ones[:, 0:1], mask[:, 0, :], start=True, stop=False)
            pe.matmul(bank[6][0:1, 0:NE], ones[:, 0:1], mask[:, 1, :], start=False, stop=True).then_inc(pos_done, 1)

            def gather(e):
                for half in range(2):
                    for k in range(4):
                        for t in range(TT):
                            rows = pick[:, bass.ds(e, 1), t, :].rearrange("p e c -> p (e c)")
                            kk = half * 4 + k
                            ins = pe.matmul(bank[4 + half][:, k * CAP:(k + 1) * CAP], h[:, t, kk * P:(kk + 1) * P],
                                            rows, start=(t == 0), stop=(t == TT - 1))
                    ins.then_inc(gather_done, 1)

            def scatter(i):
                pe.wait_ge(spread_ready, i + 1)
                pe.wait_ge(y_copied, 2 * i + 2)
                for item in range(4):
                    t, half = item // 2, item % 2
                    pe.matmul(bank[SCATTER_BANKS[item]][:, :], spread[:, t * P:(t + 1) * P],
                              y_sb[:, half * 512:(half + 1) * 512], start=True, stop=True).then_inc(scatter_done, 1)

            def expert(pass_no, e, last):
                trip = moe_trip(pass_no, e)
                i = e + (NE + 1) * pass_no
                pe.wait_ge(hg_ready, per_trip(trip, 2) + 2)

                def spread_gates():
                    pe.wait_ge(gated_ready, per_trip(trip, 2) + 2)
                    pe.wait_ge(scatter_added, 4 * i + 4)
                    for t in range(TT):
                        ins = pe.transpose(bank[1][:, t * P:(t + 1) * P], gated[:, t, :], ident)
                    ins.then_inc(spread_done, 1)

                def next_gather():
                    pe.wait_ge(spread_ready, i + 2)
                    gather(e + 1)

                behind = {SCATTER: lambda: scatter(i), SPREAD: spread_gates}
                if not last:
                    behind[down_tile(NG - 2) + 1] = next_gather
                swiglu(FFN0[1], trip, 1, hg_hi, hg_lo, bank[6:8], behind)

            def experts(pass_no):
                pe.wait_ge(pick_ready, TT * (pass_no + 1))
                gather(0)
                with pe.Fori(0, NE - 1) as e:
                    expert(pass_no, e, False)
                expert(pass_no, NE - 1, True)
                scatter((NE + 1) * pass_no + NE)

            pe.wait_ge(counts_ready, 1)
            experts(0)
            most = pe.value_load(counts[0:1, NE:NE + 1], min_val=0, max_val=S)
            with pe.If(most > CAP):
                experts(1)
                pe.nop()


NAMES = ["x"] + [f"l{l}_{n}" for l in range(2) for n in ("norm_mix", "w_in", "b_f", "mix_gain", "w_out", "norm_ffn")] + [
    "l0_w1", "l0_w3", "l0_w2", "l1_w_router", "l1_we1", "l1_we3", "l1_we2", "final_norm"]


def constants():
    import numpy as np
    c = np.zeros((P, C_END), np.float32)
    r = np.arange(P)
    c[:, C_ID:C_ID + P] = np.eye(P)
    c[:, C_LT:C_LT + P] = r[:, None] < r[None, :]
    c[:, C_ONE:C_ONE + P] = 1.0
    c[:, C_IOTA:C_IOTA + P] = r[None, :]
    for j, (q0, k0) in enumerate(((0, 0), (P, 0), (P, P))):
        dist = (q0 + r[:, None]) - (k0 + r[None, :])
        causal = dist >= 0
        times = sum(((dist % dil == 0) & causal & (dist <= win // dil * dil)).astype(int)
                    for win, dil in ((128, 1), (512, 4), (2048, 16)))
        sl = slice(j * P, (j + 1) * P)
        c[:, C_CAUSAL:C_CAUSAL + TRI][:, sl] = np.where(causal, 0.0, -1e30)
        c[:, C_UNION:C_UNION + TRI][:, sl] = np.where(times > 0, 0.0, -1e30)
        c[:, C_MULT:C_MULT + TRI][:, sl] = times
    inv = np.float32(500000.0) ** (-np.arange(0, ROT, 2, dtype=np.float32) / np.float32(ROT))
    ang = np.arange(S, dtype=np.float32)[:, None] * inv[None, :].astype(np.float32)
    for t in range(TT):
        c[:, C_COS + t * HALF:C_COS + (t + 1) * HALF] = np.cos(ang[t * P:(t + 1) * P])
        c[:, C_SIN + t * HALF:C_SIN + (t + 1) * HALF] = np.sin(ang[t * P:(t + 1) * P])
    for hh in range(H_FOX):
        c[hh, C_SEL + hh * P:C_SEL + (hh + 1) * P] = 1.0
    return c


def kernel(**inputs):
    import numpy as np
    import concourse.bacc as bacc
    from concourse.bass_utils import run_bass_kernel_spmd

    nc = bacc.Bacc("TRN2", target_bir_lowering=False, num_devices=1)
    arrays, args = {}, {}
    given = {name: np.ascontiguousarray(inputs[name]) for name in NAMES}
    given["const"] = constants()
    for name, v in given.items():
        arrays[f"in_{name}"] = v
        args[name] = nc.dram_tensor(f"in_{name}", v.shape, mybir.dt.from_np(v.dtype), kind="ExternalInput").ap()
    out = nc.dram_tensor("out", (1, S, D), F32, kind="ExternalOutput").ap()
    hybrid_trunk(nc, args, out)
    r = run_bass_kernel_spmd(nc, [arrays], core_ids=[0])
    return r.results[0]["out"]
```

```python
import concourse.bass as bass
from concourse import mybir
from contextlib import ExitStack

F32 = mybir.dt.float32
F32R = mybir.dt.float32r
I32 = mybir.dt.int32
U32 = mybir.dt.uint32
ALU = mybir.AluOpType
ACT = mybir.ActivationFunctionType
AX = mybir.AxisListType.X

P = 128
D = 1024
S = 256
HD = 64
NH = 16
H_FOX = 5
H_MOBA = 5
F = 3584
NE = 8
EPS = 1e-6
TT = S // P
KD = D // P
ROT = HD // 4
HALF = ROT // 2
WIDE = 512
GROUP = WIDE
CH = GROUP // P
NG = F // GROUP
RAW_SLOTS = 6
CUT_SLOTS = 7
KT = KD // 2
TILE = KT * WIDE
HALF_TILE = TILE // 2
CT = TILE // D
PER_FFN = 6 * NG
MIX_TILES = 16
CAP = P
SCATTER_BANKS = (1, 3, 4, 5)
SCATTER, SPREAD = 3, 21
TRI = 3 * P
GROUPS = ((0, H_FOX * HD), (H_FOX * HD, (H_FOX + H_MOBA) * HD), ((H_FOX + H_MOBA) * HD, D))

C_ID, C_LT, C_ONE, C_IOTA = 0, 128, 256, 384
C_CAUSAL = C_IOTA + P + 1
C_UNION, C_MULT = C_CAUSAL + TRI, C_CAUSAL + 2 * TRI
C_COS = C_CAUSAL + 3 * TRI
C_SIN = C_COS + TT * HALF
C_SEL = C_SIN + TT * HALF
C_END = C_SEL + H_FOX * P

BLOCKS = (("qk", 0), ("v", 0), ("qk", 1), ("qk", 2), ("qk", 3), ("v", 1))
PROJ_HALVES = 4 * len(BLOCKS)
HB = 4
STEPS = {1: [("forget", 0)], 3: [("turn_forget", 0)], 5: [("bias", 0), ("turn", 0)], 6: [("scores", 0)], 7: [("scores", 1)],
         8: [("probs", 0), ("scores", 2)], 9: [("probs", 1), ("scores", 3), ("values", 0)],
         10: [("probs", 2), ("values", 1)], 11: [("probs", 3), ("values", 2)], 12: [("values", 3)],
         13: [("turn", 1)], 14: [("scores", 4)], 15: [("scores", 5), ("probs", 4)],
         16: [("scores", 6), ("probs", 5), ("values", 4)], 17: [("scores", 7), ("probs", 6), ("values", 5)],
         18: [("turn", 2), ("probs", 7), ("values", 6)], 19: [("scores", 8), ("scores", 9), ("values", 7)],
         20: [("probs", 8), ("probs", 9), ("scores", 10), ("scores", 11)],
         21: [("turn", 3), ("probs", 10), ("probs", 11)], 22: [("scores", 12), ("scores", 13)],
         23: [("probs", 12), ("probs", 13), ("scores", 14), ("scores", 15)],
         24: [("values", 8), ("values", 9), ("probs", 14), ("probs", 15), ("values", 10), ("values", 11)],
         25: [("values", 12), ("values", 13), ("values", 14), ("values", 15)]}


def steps(s, kind):
    return [i for k, i in STEPS.get(s, ()) if k == kind]


def up_tile(g):
    return 0 if g == 0 else 6 * g - 2


def down_tile(g):
    return 6 * g + 8 if g < NG - 1 else PER_FFN - 2


def ffn_order():
    order = [None] * PER_FFN
    for g in range(NG):
        for half in range(2):
            order[up_tile(g) + half] = ("w1", g, half)
            order[up_tile(g) + 2 + half] = ("w3", g, half)
            order[down_tile(g) + half] = ("w2", g, half)
    return order


def hybrid_trunk(nc, a, out):
    ctx = ExitStack()
    with ctx:
        def sb(name, shape, dt=F32):
            return ctx.enter_context(nc.sbuf_tensor(name, shape, dt))

        def sem(name):
            return ctx.enter_context(nc.semaphore(name))

        raw = sb("raw", [P, RAW_SLOTS, TILE])
        w_hi = sb("w_hi", [P, CUT_SLOTS, HALF_TILE], F32R)
        w_lo = sb("w_lo", [P, CUT_SLOTS, HALF_TILE], F32R)
        const = sb("const", [P, C_END])
        x = sb("x_res", [P, TT, D])
        h = sb("h_tok", [P, TT, D])
        hT_hi = sb("hT_hi", [P, KD, S], F32R)
        hT_lo = sb("hT_lo", [P, KD, S], F32R)
        gain = sb("gain", [P, D])
        work = sb("work", [P, TT * 3 * D + 2 * KD * S])
        hid = sb("hid", [P, TT, GROUP])
        hidT_hi = sb("hidT_hi", [P, TT, CH * P], F32R)
        hidT_lo = sb("hidT_lo", [P, TT, CH * P], F32R)
        probsT = sb("probsT", [P, 2, TRI])
        wf = sb("w_forget", [P, KD, H_FOX])
        bf = sb("b_forget", [H_FOX, 1])
        wr = sb("w_router", [P, KD, NE])
        rope_t1 = sb("rope_t1", [P, 4 * HB * HALF])
        wf_cut = sb("w_forget_cut", [P, KD, 2, H_FOX], F32R)
        wr_cut = sb("w_router_cut", [P, KD, 2, NE], F32R)
        small = sb("small", [P, 320])
        idx8 = sb("idx8", [P, TT, 8], U32)
        counts = sb("counts", [1, 16], I32)

        ident = const[:, C_ID:C_ID + P]
        before = const[:, C_LT:C_LT + P]
        ones = const[:, C_ONE:C_ONE + P]
        iota = const[:, C_IOTA:C_IOTA + NE]
        place = const[:, C_IOTA + 1:C_IOTA + 1 + CAP]
        qkv = work[:, 0:TT * 3 * D].rearrange("p (t n) -> p t n", t=TT)
        qkT = work[:, TT * 3 * D:].rearrange("p (c t) -> p c t", c=2 * KD)
        o_tok = qkv[:, :, 0:D]
        fox_bias = h[:, :, :].rearrange("p t d -> p (t d)")[:, 0:H_FOX * TRI].rearrange("p (h n) -> p h n", h=H_FOX)
        probs = hid[:, :, 0:TRI]

        def probsT_of(hh):
            if hh < NH // 2 or hh >= NH - 2:
                return probsT[:, hh % 2, :]
            if hh == NH - 3:
                return qkT[:, 0:2, :].rearrange("p c t -> p (c t)")[:, 0:TRI]
            return fox_bias[:, hh - NH // 2, :]

        o = 0
        pick = work[:, o:o + NE * TT * CAP].rearrange("p (e t c) -> p e t c", e=NE, t=TT)
        o += NE * TT * CAP
        gated = work[:, o:o + TT * CAP].rearrange("p (t c) -> p t c", t=TT)
        o += TT * CAP
        spread = work[:, o:o + S]
        o += S
        y_sb = work[:, o:o + D]
        hg_hi = hT_hi[:, :, 0:CAP]
        hg_lo = hT_lo[:, :, 0:CAP]
        ss = small[:, 0:8]
        rstd = small[:, 8:16]
        newton = small[:, 306:314]
        rstd_x = small[:, 314:316]
        expert_rows = y_sb[0:2 * NE, 0:S]
        square = hid[:, :, :].rearrange("p t n -> p (t n)")
        forget_tok = small[:, 256:256 + TT * H_FOX].rearrange("p (t h) -> p t h", t=TT)
        negmax = small[:, 16:48].rearrange("p (h t) -> p h t", t=TT)
        rowmax = small[:, 48:80].rearrange("p (h t) -> p h t", t=TT)
        rowsum = small[:, 80:112].rearrange("p (t h) -> p t h", t=TT)
        rinv = small[:, 112:144].rearrange("p (t h) -> p t h", t=TT)
        cT = small[:, 144:144 + TT * H_FOX].rearrange("p (t h) -> p t h", t=TT)
        lg = small[:, 160:176].rearrange("p (t e) -> p t e", t=TT)
        top = small[:, 176:192].rearrange("p (t e) -> p t e", t=TT)
        idf = small[:, 192:208].rearrange("p (t e) -> p t e", t=TT)
        pick0 = small[:, 208:224].rearrange("p (t e) -> p t e", t=TT)
        pick1 = small[:, 224:240].rearrange("p (t e) -> p t e", t=TT)
        mask = small[:, 240:256].rearrange("p (t e) -> p t e", t=TT)
        gate = small[:, 256:272].rearrange("p (t e) -> p t e", t=TT)
        pos = small[:, 272:288].rearrange("p (t e) -> p t e", t=TT)
        dz = small[:, 288:290]
        z = small[:, 290:292]
        den = small[:, 292:294]
        g0 = small[:, 294:296]
        g1 = small[:, 296:298]
        cnt_f = small[0:1, 298:306]
        fox = probsT[0:H_FOX, :, :].rearrange("h b n -> h (b n)")[:, 0:2 * S].rearrange("h (r t) -> h r t", r=2)
        rope_t = (h[:, :, :].rearrange("p t d -> p (t d)")[:, H_FOX * TRI:H_FOX * TRI + 4 * HB * HALF],
                  rope_t1[:, :])

        bank = [ctx.enter_context(nc.psum_tensor(f"bank{i}", [P, 512], F32)) for i in range(8)]

        const_in, x_in, small_in = sem("const_in"), sem("x_in"), sem("small_in")
        wf_in = sem("wf_in")
        gain_in = sem("gain_in")
        tile_in = [sem(f"tile_in{i}") for i in range(RAW_SLOTS)]
        hi_done, cut_done, half_used = sem("hi_done"), sem("cut_done"), sem("half_used")
        h_ready = sem("h_ready")
        y_ready = sem("y_ready")
        var_ready, root_ready, rstd_ready = sem("var_ready"), sem("root_ready"), sem("rstd_ready")
        h_scaled = sem("h_scaled")
        logits_done, logits_copied = sem("logits_done"), sem("logits_copied")
        forget_tok_done, forget_tok_ready = sem("forget_tok_done"), sem("forget_tok_ready")
        tr_done = sem("tr_done")
        hT_hi_done, hT_done = sem("hT_hi_done"), sem("hT_done")
        wf_hi_done, wf_cut_done, wr_hi_done, wr_cut_done = (sem("wf_hi_done"), sem("wf_cut_done"),
                                                            sem("wr_hi_done"), sem("wr_cut_done"))
        forget_done, forget_ln, c_ready = sem("forget_done"), sem("forget_ln"), sem("c_ready")
        proj_by_act, proj_by_dve = sem("proj_by_act"), sem("proj_by_dve")
        bias_done, bias_ready = sem("bias_done"), sem("bias_ready")
        rope_by_dve, rope_by_pool = sem("rope_by_dve"), sem("rope_by_pool")
        pool_chain = sem("pool_chain")
        qk_tr_done, qkT_by_act, qkT_by_dve = sem("qk_tr_done"), sem("qkT_by_act"), sem("qkT_by_dve")
        scores_done, logits_ready, exp_done, weighted = (sem("scores_done"), sem("logits_ready"),
                                                         sem("exp_done"), sem("weighted"))
        probs_tr_done, probsT_ready, pv_done, o_ready = (sem("probs_tr_done"), sem("probsT_ready"),
                                                         sem("pv_done"), sem("o_ready"))
        silu_done, hid_done = sem("silu_done"), sem("hid_done")
        hid_tr_done, hidT_hi_done, hidT_done = sem("hid_tr_done"), sem("hidT_hi_done"), sem("hidT_done")
        router_done, top_ready, z_ready, mask_ready = (sem("router_done"), sem("top_ready"),
                                                       sem("z_ready"), sem("mask_ready"))
        pos_done, counts_ready = sem("pos_done"), sem("counts_ready")
        pick_ready = sem("pick_ready")
        gather_done, hg_hi_done, hg_ready = sem("gather_done"), sem("hg_hi_done"), sem("hg_ready")
        scatter_done, scatter_added = sem("scatter_done"), sem("scatter_added")
        gated_ready, spread_done, spread_ready = sem("gated_ready"), sem("spread_done"), sem("spread_ready")
        y_copied = sem("y_copied")
        out_by_act, out_by_dve, out_stored = sem("out_by_act"), sem("out_by_dve"), sem("out_stored")
        act_chain = sem("act_chain")
        dve_chain, dve_chain_pass, dve_chain_end = sem("dve_chain"), sem("dve_chain_pass"), sem("dve_chain_end")

        def linker(eng, s):
            n = [0]

            def link(ins):
                n[0] += 1
                ins.then_inc(s, 1)
                eng.wait_ge(s, n[0])
            return link

        MIX0 = (0, MIX_TILES + PER_FFN)
        FFN0 = (MIX_TILES, 2 * MIX_TILES + PER_FFN)

        silu_before_cut = {2 * (up_tile(g) + 2) + CUT_SLOTS - 1: g for g in range(NG)}
        mult_before_cut = {2 * (up_tile(g) + 4) + CUT_SLOTS - 1: g for g in range(NG)}
        hid_before_cut = {2 * (up_tile(g + 1) + 1 if g + 1 < NG else down_tile(g)) + CUT_SLOTS: g for g in range(NG)}

        def per_trip(trip, step):
            return 0 if isinstance(trip, int) and trip == 0 else trip * step

        def turned(stage, b):
            return bank[(4, 5, 2, 3)[b] if stage % 3 == 0 else 4 + b]

        def halves(n):
            return (2 * n, 2 * n + 1)

        def raw_half(m):
            n = m // 2
            return raw[:, n % RAW_SLOTS, (m % 2) * HALF_TILE:(m % 2 + 1) * HALF_TILE]

        split_tiles = [n0 + 2 * beta + half for n0 in MIX0 for beta, (kind, _) in enumerate(BLOCKS) if kind == "qk"
                       for half in range(2)]

        def transfers(n):
            return n // RAW_SLOTS + 1 + sum(1 for i in split_tiles if i <= n and i % RAW_SLOTS == n % RAW_SLOTS)

        def cut_hi(act, m, trip=0):
            n = m // 2
            act.wait_ge(tile_in[n % RAW_SLOTS], 16 * transfers(n) + per_trip(trip, 16 * (PER_FFN // RAW_SLOTS)))
            if m >= CUT_SLOTS:
                act.wait_ge(half_used, m - CUT_SLOTS + 1 + per_trip(trip, 2 * PER_FFN))
            act.copy(w_hi[:, m % CUT_SLOTS, :], raw_half(m)).then_inc(hi_done, 1)

        def cut_lo(dve, m, trip=0):
            dve.wait_ge(hi_done, m + 1 + per_trip(trip, 2 * PER_FFN))
            dve.tensor_tensor(w_lo[:, m % CUT_SLOTS, :], raw_half(m), w_hi[:, m % CUT_SLOTS, :].bitcast(F32),
                              ALU.subtract).then_inc(cut_done, 1)

        def block_out(beta, t):
            kind, b = BLOCKS[beta]
            if kind == "v":
                return qkv[:, t, 2 * D + b * WIDE:2 * D + (b + 1) * WIDE], bank[t][:, :]
            return (qkv[:, t, 0:2 * D].rearrange("p (s n) -> p s n", s=2)[:, :, b * HB * HD:(b + 1) * HB * HD],
                    bank[t][:, :].rearrange("p (s n) -> p s n", s=2))

        def rotate(eng, link, b, t, done):
            h0 = max(HB * b, H_FOX)
            n = HB * (b + 1) - h0
            qk = qkv[:, t, 0:2 * D].rearrange("p (s h d) -> p s h d", s=2, h=NH)[:, :, h0:h0 + n, :]
            x1, x2 = qk[:, :, :, 0:HALF], qk[:, :, :, HALF:ROT]
            cs, sn = (const[:, c0 + t * HALF:c0 + (t + 1) * HALF].unsqueeze(1).unsqueeze(1)
                      .to_broadcast([P, 2, n, HALF]) for c0 in (C_COS, C_SIN))
            ta, tb = (rope_t[t][:, u * 2 * n * HALF:(u + 1) * 2 * n * HALF]
                      .rearrange("p (s h d) -> p s h d", s=2, h=n) for u in range(2))
            link(eng.tensor_tensor(ta, x2, sn, ALU.mult))
            link(eng.tensor_tensor(tb, x1, sn, ALU.mult))
            link(eng.tensor_tensor(x1, x1, cs, ALU.mult))
            link(eng.tensor_tensor(x2, x2, cs, ALU.mult))
            link(eng.tensor_tensor(x1, x1, ta, ALU.subtract))
            eng.tensor_tensor(x2, x2, tb, ALU.add).then_inc(done, 1)

        def moe_trip(pass_no, e):
            return e + NE * pass_no

        block = ctx.enter_context(nc.Block())

        @block.sync
        def _(sp):
            def load(n, src, trip=0):
                if n >= RAW_SLOTS:
                    sp.wait_ge(cut_done, 2 * (n - RAW_SLOTS + 1) + per_trip(trip, 2 * PER_FFN))
                if len(src.shape) == 4:
                    shaped = raw[:, n % RAW_SLOTS, :].rearrange("p (k s c) -> p k s c", k=src.shape[1], s=2)
                    for u in range(2):
                        sp.dma_start(shaped[:, :, u, :], src[:, :, u, :]).then_inc(tile_in[n % RAW_SLOTS], 16)
                else:
                    shaped = raw[:, n % RAW_SLOTS, :].rearrange("p (k c) -> p k c", k=src.shape[1])
                    sp.dma_start(shaped, src).then_inc(tile_in[n % RAW_SLOTS], 16)

            def d_tile(w, c, half):
                return w[half * D // 2:(half + 1) * D // 2, c * WIDE:(c + 1) * WIDE].rearrange("(k p) n -> p k n", p=P)

            def block_tile(w, kind, b, half):
                if kind == "v":
                    return d_tile(w, 2 * D // WIDE + b, half)
                rows = w[half * D // 2:(half + 1) * D // 2, 0:2 * D]
                return rows.rearrange("(k p) (s n) -> p k s n", p=P, s=2)[:, :, :, b * HB * HD:(b + 1) * HB * HD]

            def swiglu_src(kind, g, half, w1, w3, w2):
                if kind == "w2":
                    r0 = (2 * g + half) * CT * P
                    return w2[r0:r0 + CT * P, :].rearrange("(c p) n -> p c n", p=P)
                return d_tile(w1 if kind == "w1" else w3, g, half)

            sp.dma_start(x[:, :, :], a["x"].rearrange("b (t p) d -> p (b t) d", p=P)).then_inc(x_in, 16)
            sp.dma_start(const[:, :], a["const"]).then_inc(const_in, 16)
            sp.dma_start(wf[:, :, :], a["l0_w_in"][:, 3 * D:].rearrange("(k p) n -> p k n", p=P)).then_inc(wf_in, 16)
            sp.dma_start(bf[:, :], a["l0_b_f"].rearrange("(h o) -> h o", o=1)).then_inc(wf_in, 16)
            sp.dma_start(wr[:, :, :], a["l1_w_router"].rearrange("(k p) n -> p k n", p=P)).then_inc(small_in, 16)
            for layer in range(2):
                n = MIX0[layer]
                for kind, b in BLOCKS:
                    for half in range(2):
                        load(n, block_tile(a[f"l{layer}_w_in"], kind, b, half))
                        n += 1
                for c in range(D // WIDE):
                    for half in range(2):
                        load(n, d_tile(a[f"l{layer}_w_out"], c, half))
                        n += 1
                if layer == 0:
                    sp.wait_ge(c_ready, 1)
                    sp.dma_start(wf[:, :, :], a["l1_w_in"][:, 3 * D:].rearrange("(k p) n -> p k n", p=P)
                                 ).then_inc(wf_in, 16)
                    sp.dma_start(bf[:, :], a["l1_b_f"].rearrange("(h o) -> h o", o=1)).then_inc(wf_in, 16)
                if layer == 0:
                    for j, (kind, g, half) in enumerate(ffn_order()):
                        load(FFN0[0] + j, swiglu_src(kind, g, half, a["l0_w1"], a["l0_w3"], a["l0_w2"]))

            def experts(pass_no):
                with sp.Fori(0, NE) as e:
                    ws = [a[k][bass.ds(e, 1), :, :].rearrange("e r c -> (e r) c") for k in ("l1_we1", "l1_we3", "l1_we2")]
                    for j, (kind, g, half) in enumerate(ffn_order()):
                        load(FFN0[1] + j, swiglu_src(kind, g, half, *ws), moe_trip(pass_no, e))

            experts(0)
            sp.wait_ge(counts_ready, 1)
            most = sp.value_load(counts[0:1, NE:NE + 1], min_val=0, max_val=S)
            with sp.If(most > CAP):
                experts(1)
                sp.nop()
            for t in range(TT):
                sp.wait_ge(out_by_dve if t else out_by_act, 1)
                sp.dma_start(out[0, t * P:(t + 1) * P, :], h[:, t, :]).then_inc(out_stored, 16)
            sp.wait_ge(out_stored, 16 * TT)

        @block.gpsimd
        def _(pool):
            order = ("l0_norm_mix", "l0_mix_gain", "l0_norm_ffn", "l1_norm_mix", "l1_mix_gain", "l1_norm_ffn",
                     "final_norm")
            freed = ((h_ready, 4), (y_ready, 2), (h_ready, 8), (h_ready, 12), (y_ready, 4), (h_ready, 16))
            link = linker(pool, pool_chain)
            for i, name in enumerate(order):
                if i:
                    pool.wait_ge(*freed[i - 1])
                pool.dma_start(gain[:, :], a[name].partition_broadcast(P)).then_inc(gain_in, 16)
                if i in (1, 4):
                    if i == 1:
                        pool.wait_ge(const_in, 16)
                    for beta, (kind, b) in enumerate(BLOCKS):
                        if kind == "qk" and b:
                            pool.wait_ge(proj_by_dve, 6 * (i // 3) + beta + 1)
                            rotate(pool, link, b, 1, rope_by_pool)

        @block.scalar
        def _(act):
            link = linker(act, act_chain)

            def copy_transposed(stage, banks=range(4)):
                for b in banks:
                    act.wait_ge(tr_done, 4 * stage + b + 1)
                    act.copy(hT_hi[:, 2 * b:2 * b + 2, :], turned(stage, b)[:, :].rearrange("p (k t) -> p k t", k=2)
                             ).then_inc(hT_hi_done, 1)

            def root(norm_no, r):
                act.wait_ge(var_ready, norm_no + 1)
                link(act.activation(r, ss[:, 0:r.shape[1]], ACT.Ln))
                act.activation(r, r, ACT.Exp, scale=-0.5).then_inc(root_ready, 1)

            def mixer(layer):
                n0 = MIX0[layer]
                if not layer:
                    root(0, rstd_x)
                act.wait_ge(wf_in, 32 * (layer + 1))
                act.copy(wf_cut[:, :, 0, :], wf[:, :, :]).then_inc(wf_hi_done, 1)
                if not layer:
                    for m in halves(0):
                        cut_hi(act, m)
                copy_transposed(3 * layer)
                if not layer:
                    for m in halves(1):
                        cut_hi(act, m)
                    act.wait_ge(small_in, 16)
                    act.copy(wr_cut[:, :, 0, :], wr[:, :, :]).then_inc(wr_hi_done, 1)
                else:
                    root(3, rstd_x)
                for s in range(4, CUT_SLOTS):
                    cut_hi(act, 2 * n0 + s)

                def forget_logarithm():
                    act.wait_ge(forget_done, layer + 1)
                    link(act.activation(fox[:, 0, :], bank[4][0:H_FOX, 0:S], ACT.Identity, bias=bf[:, :]))
                    link(act.activation(fox[:, 1, :], fox[:, 0, :], ACT.Abs))
                    link(act.activation(fox[:, 1, :], fox[:, 1, :], ACT.Exp, scale=-1.0))
                    act.activation(fox[:, 1, :], fox[:, 1, :], ACT.Ln, bias=1.0).then_inc(forget_ln, 1)

                def exps(hh):
                    act.wait_ge(logits_ready, NH * layer + hh + 1)
                    for t in range(TT):
                        lo, hi = (0, P) if t == 0 else (P, TRI)
                        row = probs[:, hh % 2, lo:hi]
                        ins = act.activation(row, row, ACT.Exp, bias=negmax[:, hh, t:t + 1],
                                             accum_out=rowsum[:, t, hh:hh + 1])
                    ins.then_inc(exp_done, 1)

                def copy_probsT(hh):
                    act.wait_ge(probs_tr_done, NH * layer + hh + 1)
                    if 2 <= hh < NH // 2:
                        act.wait_ge(pv_done, NH * layer + hh - 1)
                    elif hh >= NH // 2:
                        act.wait_ge(pv_done, NH * layer + NH // 2)
                    act.copy(probsT_of(hh), bank[4 + hh % 2][:, 0:TRI]).then_inc(probsT_ready, 1)

                for s in range(max(STEPS) + 1):
                    if s < PROJ_HALVES:
                        if s % 4 == 3:
                            act.wait_ge(half_used, 2 * n0 + s + 1)
                            act.wait_ge(rstd_ready, 3 * layer + 1)
                            act.activation(*block_out(s // 4, 0), ACT.Copy, scale=rstd_x[:, 0:1]
                                           ).then_inc(proj_by_act, 1)
                        cut_hi(act, 2 * n0 + s + CUT_SLOTS)
                    if s == 3:
                        forget_logarithm()
                    for b in steps(s, "turn"):
                        act.wait_ge(qk_tr_done, 2 * (4 * layer + b) + 1)
                        act.activation(qkT[:, 2 * b:2 * b + 2, :], bank[2][:, :].rearrange("p (c t) -> p c t", c=2),
                                       ACT.Copy, scale=HD ** -0.5).then_inc(qkT_by_act, 1)
                    for hh in steps(s, "probs"):
                        copy_probsT(hh)
                    for hh in steps(s, "scores"):
                        exps(hh)
                root(3 * layer + 1, rstd[:, 0:3 * TT])
                copy_transposed(3 * layer + 1)
                for m in halves(n0 + 15)[1:] + halves(FFN0[layer]) + halves(FFN0[layer] + 1):
                    cut_hi(act, m)
                act.wait_ge(half_used, 2 * n0 + 30)
                copy_transposed(3 * layer + 2, (0, 1))

            def silu(g, trip, tokens):
                n = FFN0[0 if tokens == TT else 1]
                act.wait_ge(half_used, 2 * (n + up_tile(g) + 2) + per_trip(trip, 2 * PER_FFN))
                for t in range(tokens):
                    scale = rstd_x[:, t:t + 1] if tokens == TT else 1.0
                    act.activation(hid[:, t, :], bank[t][:, :], ACT.Silu, scale=scale).then_inc(silu_done, 1)

            def hid_hi(count, trip, tokens):
                for t in range(tokens):
                    act.wait_ge(hid_tr_done, count + t + 1 + per_trip(trip, NG))
                    act.copy(hidT_hi[:, t, :], bank[2 + t][:, :]).then_inc(hidT_hi_done, 1)

            mixer(0)
            n0 = FFN0[0]
            copy_transposed(2, (2, 3))
            root(2, rstd_x)
            act.wait_ge(rstd_ready, 3)
            for m in range(4, 2 * PER_FFN + 4):
                if m in hid_before_cut:
                    hid_hi(TT * hid_before_cut[m], 0, TT)
                if m in silu_before_cut:
                    silu(silu_before_cut[m], 0, TT)
                cut_hi(act, 2 * n0 + m)
            mixer(1)
            copy_transposed(5, (2, 3))
            for m in (4, 5):
                cut_hi(act, 2 * FFN0[1] + m)
            root(5, rstd_x)
            act.wait_ge(rstd_ready, 6)
            for t in range(TT):
                act.activation(h[:, t, :], h[:, t, :], ACT.Copy, scale=rstd_x[:, t:t + 1]).then_inc(h_scaled, 1)
            act.wait_ge(top_ready, 1)
            act.activation(z, dz, ACT.Exp).then_inc(z_ready, 1)
            cut_hi(act, 2 * FFN0[1] + 6)

            def gathered_hi(trip):
                for half in range(2):
                    act.wait_ge(gather_done, per_trip(trip, 2) + half + 1)
                    act.copy(hg_hi[:, half * 4:half * 4 + 4, :], bank[4 + half][:, :].rearrange("p (k c) -> p k c", k=4)
                             ).then_inc(hg_hi_done, 1)

            def expert(pass_no, e, last):
                trip = moe_trip(pass_no, e)
                for m in range(CUT_SLOTS, 2 * PER_FFN + CUT_SLOTS):
                    if m in hid_before_cut:
                        hid_hi(TT * NG + hid_before_cut[m], trip, 1)
                        if hid_before_cut[m] == NG - 1 and not last:
                            gathered_hi(trip + 1)
                    if m in silu_before_cut:
                        silu(silu_before_cut[m], trip, 1)
                    if m < 2 * PER_FFN + CUT_SLOTS - 1 and not (last and m >= 2 * PER_FFN):
                        cut_hi(act, 2 * FFN0[1] + m, trip)
                act.wait_ge(half_used, 2 * (FFN0[1] + PER_FFN) + per_trip(trip, 2 * PER_FFN))
                for half in range(2):
                    act.copy(y_sb[:, half * 512:(half + 1) * 512], bank[6 + half][:, :]).then_inc(y_copied, 1)
                if not last:
                    cut_hi(act, 2 * (FFN0[1] + PER_FFN) + CUT_SLOTS - 1, trip)

            def experts(pass_no):
                if pass_no:
                    for m in range(CUT_SLOTS):
                        cut_hi(act, 2 * FFN0[1] + m, moe_trip(pass_no, 0))
                gathered_hi(moe_trip(pass_no, 0))
                with act.Fori(0, NE - 1) as e:
                    expert(pass_no, e, False)
                expert(pass_no, NE - 1, True)

            experts(0)
            act.wait_ge(counts_ready, 1)
            most = act.value_load(counts[0:1, NE:NE + 1], min_val=0, max_val=S)
            with act.If(most > CAP):
                experts(1)
                act.nop()
            root(6, rstd_x)
            act.wait_ge(rstd_ready, 7)
            act.activation(h[:, 0, :], h[:, 0, :], ACT.Copy, scale=rstd_x[:, 0:1]).then_inc(out_by_act, 1)

        @block.vector
        def _(dve):
            link = linker(dve, dve_chain)

            def await_gain(i):
                dve.wait_ge(gain_in, 16 * (i + 1))
                return gain[:, :]

            def variance(norm_no, n):
                dve.tensor_scalar(ss[:, 0:n], ss[:, 0:n], EPS, None, ALU.add).then_inc(var_ready, 1)

            def inverse_root(norm_no, r, link):
                n = r.shape[1]
                dve.wait_ge(root_ready, norm_no + 1)
                link(dve.tensor_tensor(newton[:, 0:n], r, r, ALU.mult))
                link(dve.tensor_tensor(newton[:, 0:n], newton[:, 0:n], ss[:, 0:n], ALU.mult))
                link(dve.tensor_scalar(newton[:, 0:n], newton[:, 0:n], -0.5, 1.5, ALU.mult, ALU.add))
                dve.tensor_tensor(r, r, newton[:, 0:n], ALU.mult).then_inc(rstd_ready, 1)
                dve.wait_ge(rstd_ready, norm_no + 1)

            def sum_squares(t, link):
                link(dve.tensor_tensor_reduce(out=square, in0=x[:, t, :], in1=x[:, t, :], scale=1.0 / D, scalar=0.0,
                                              op0=ALU.mult, op1=ALU.add, accum_out=ss[:, t:t + 1]))

            def gained(gain_no, t, half):
                cols = slice(half * WIDE, (half + 1) * WIDE)
                dve.tensor_tensor(h[:, t, cols], x[:, t, cols], await_gain(gain_no)[:, cols], ALU.mult
                                  ).then_inc(h_ready, 1)

            def norm_products(norm_no, banks, behind=()):
                sum_squares(0, link)
                copy_transposed(norm_no, banks)
                sum_squares(1, link)
                variance(norm_no, TT)
                for m in behind:
                    cut_lo(dve, m)
                inverse_root(norm_no, rstd_x, link)

            def final_norm(link):
                for t in range(TT):
                    sum_squares(t, link)
                variance(6, TT)
                g = await_gain(6)
                for t in range(TT):
                    link(dve.tensor_tensor(h[:, t, :], x[:, t, :], g, ALU.mult))
                inverse_root(6, rstd_x, link)
                dve.tensor_scalar(h[:, 1, :], h[:, 1, :], rstd_x[:, 1:2], None, ALU.mult).then_inc(out_by_dve, 1)

            def copy_transposed(stage, banks=range(4)):
                for b in banks:
                    dve.wait_ge(hT_hi_done, 4 * stage + b + 1)
                    dve.tensor_tensor(hT_lo[:, 2 * b:2 * b + 2, :], turned(stage, b)[:, :].rearrange("p (k t) -> p k t", k=2),
                                      hT_hi[:, 2 * b:2 * b + 2, :].bitcast(F32), ALU.subtract).then_inc(hT_done, 1)

            def mixer(layer):
                n0 = MIX0[layer]

                def cut_forget():
                    dve.wait_ge(wf_hi_done, layer + 1)
                    dve.tensor_tensor(wf_cut[:, :, 1, :], wf[:, :, :], wf_cut[:, :, 0, :].bitcast(F32), ALU.subtract
                                      ).then_inc(wf_cut_done, 1)

                if not layer:
                    for t in range(TT):
                        sum_squares(t, link)
                    variance(0, TT)
                    cut_forget()
                    for t in range(TT):
                        for half in range(2):
                            gained(0, t, half)
                    for m in halves(0):
                        cut_lo(dve, m)
                    inverse_root(0, rstd_x, link)
                    copy_transposed(0)
                    for m in halves(1):
                        cut_lo(dve, m)
                else:
                    cut_forget()
                if not layer:
                    dve.wait_ge(wr_hi_done, 1)
                    dve.tensor_tensor(wr_cut[:, :, 1, :], wr[:, :, :], wr_cut[:, :, 0, :].bitcast(F32), ALU.subtract
                                      ).then_inc(wr_cut_done, 1)
                for s in range(4, CUT_SLOTS):
                    cut_lo(dve, 2 * n0 + s)

                def forget_logits():
                    dve.wait_ge(forget_tok_done, layer + 1)
                    parts = bank[5][:, 0:TT * 2 * H_FOX].rearrange("p (t u h) -> p t u h", t=TT, u=2)
                    link(dve.tensor_copy(forget_tok, parts[:, :, 0, :]))
                    link(dve.tensor_tensor(forget_tok, forget_tok, parts[:, :, 1, :], ALU.add))
                    dve.tensor_tensor(forget_tok, forget_tok, rstd_x.unsqueeze(2).to_broadcast([P, TT, H_FOX]),
                                      ALU.mult).then_inc(forget_tok_ready, 1)

                def cumulate():
                    dve.wait_ge(forget_ln, layer + 1)
                    link(dve.tensor_scalar(fox[:, 0, :], fox[:, 0, :], 0.0, None, ALU.min))
                    link(dve.tensor_tensor(fox[:, 1, :], fox[:, 0, :], fox[:, 1, :], ALU.subtract))
                    link(dve.tensor_tensor_scan(fox[:, 0, :], ones[0:H_FOX, 0:1].to_broadcast([H_FOX, S]),
                                                fox[:, 1, :], 0.0, ALU.mult, ALU.add))
                    dve.tensor_scalar(fox[:, 1, :], fox[:, 0, :], -1.0, None, ALU.mult).then_inc(c_ready, 1)

                def fox_biases(heads):
                    for hh in heads:
                        src = bank[5 + hh // 2][:, (hh % 2) * S:(hh % 2 + 1) * S]
                        for t in range(TT):
                            lo, hi = (0, P) if t == 0 else (P, TRI)
                            link(dve.scalar_tensor_tensor(out=fox_bias[:, hh, lo:hi], in0=src[:, 0:hi - lo],
                                                          scalar=cT[:, t, hh:hh + 1],
                                                          in1=const[:, C_CAUSAL + lo:C_CAUSAL + hi],
                                                          op0=ALU.add, op1=ALU.add))

                def logits(hh):
                    dve.wait_ge(scores_done, NH * layer + hh + 1)
                    if hh >= 2:
                        dve.wait_ge(probs_tr_done, NH * layer + hh - 1)
                    if hh < H_FOX:
                        bias = fox_bias[:, hh, :]
                    else:
                        c0 = C_CAUSAL if hh < H_FOX + H_MOBA else C_UNION
                        bias = const[:, c0:c0 + TRI]
                    for t in range(TT):
                        lo, hi = (0, P) if t == 0 else (P, TRI)
                        ins = dve.tensor_tensor_reduce(out=probs[:, hh % 2, lo:hi], in0=bank[2 + hh % 2][:, lo:hi],
                                                       in1=bias[:, lo:hi], scale=1.0, scalar=-3.0e38, op0=ALU.add,
                                                       op1=ALU.max, accum_out=rowmax[:, hh, t:t + 1])
                        link(ins)
                    dve.tensor_scalar(negmax[:, hh, :], rowmax[:, hh, :], -1.0, None, ALU.mult
                                      ).then_inc(logits_ready, 1)

                def weight(hh):
                    dve.wait_ge(exp_done, NH * layer + hh + 1)
                    for t in range(TT):
                        lo, hi = (0, P) if t == 0 else (P, TRI)
                        row = probs[:, hh % 2, lo:hi]
                        ins = dve.tensor_tensor_reduce(out=row, in0=row, in1=const[:, C_MULT + lo:C_MULT + hi],
                                                       scale=1.0, scalar=0.0, op0=ALU.mult, op1=ALU.add,
                                                       accum_out=rowsum[:, t, hh:hh + 1])
                        if t == 0:
                            link(ins)
                    ins.then_inc(weighted, 1)

                def divide(q4):
                    dve.wait_ge(pv_done, NH * layer + 4 * q4 + 4)
                    link(dve.reciprocal(rinv[:, :, 4 * q4:4 * q4 + 4], rowsum[:, :, 4 * q4:4 * q4 + 4]))
                    src = bank[6 + q4 % 2][:, :].rearrange("p (t h d) -> p t h d", t=TT, h=4)
                    for t in range(TT):
                        link(dve.tensor_tensor(
                            o_tok[:, t, q4 * 4 * HD:(q4 + 1) * 4 * HD].rearrange("p (h d) -> p h d", h=4),
                            src[:, t, :, :],
                            rinv[:, t, 4 * q4:4 * q4 + 4].unsqueeze(2).to_broadcast([P, 4, HD]), ALU.mult))
                    dve.sem_inc(o_ready, 1)

                def sum_outputs(i):
                    lo, hi = GROUPS[i]
                    for t in range(TT):
                        link(dve.tensor_tensor_reduce(out=square[:, 0:hi - lo], in0=o_tok[:, t, lo:hi],
                                                      in1=o_tok[:, t, lo:hi], scale=1.0 / (hi - lo), scalar=0.0,
                                                      op0=ALU.mult, op1=ALU.add,
                                                      accum_out=ss[:, 3 * t + i:3 * t + i + 1]))

                for s in range(max(STEPS) + 1):
                    for hh in steps(s, "probs"):
                        if hh >= H_FOX + H_MOBA:
                            weight(hh)
                    if s == 6:
                        dve.wait_ge(bias_done, layer + 1)
                        link(dve.tensor_copy(cT, bank[4][:, 0:TT * H_FOX].rearrange("p (t h) -> p t h", t=TT)))
                        fox_biases(range(3))
                        dve.sem_inc(bias_ready, 1)
                    if s == 8:
                        fox_biases(range(3, H_FOX))
                        dve.sem_inc(bias_ready, 1)
                    if s % 4 == 0 and 0 < s <= PROJ_HALVES:
                        kind, b = BLOCKS[s // 4 - 1]
                        if kind == "qk" and b:
                            dve.wait_ge(proj_by_act, 6 * layer + s // 4)
                            rotate(dve, link, b, 0, rope_by_dve)
                    if s < PROJ_HALVES and s % 4 == 3:
                        dve.wait_ge(half_used, 2 * n0 + s + 1)
                        dst, src = block_out(s // 4, 1)
                        dve.tensor_scalar(dst, src, rstd_x[:, 1:2], None, ALU.mult).then_inc(proj_by_dve, 1)
                    if s == 1:
                        forget_logits()
                    if s == 4:
                        cumulate()
                    for b in steps(s, "turn"):
                        dve.wait_ge(qk_tr_done, 2 * (4 * layer + b) + 2)
                        dve.tensor_copy(qkT[:, KD + 2 * b:KD + 2 * b + 2, :],
                                        bank[3][:, :].rearrange("p (c t) -> p c t", c=2)).then_inc(qkT_by_dve, 1)
                    for hh in steps(s, "scores"):
                        logits(hh)
                    for hh in steps(s, "values"):
                        if hh % 4 == 3:
                            divide(hh // 4)
                        if hh == NH - HB - 1:
                            sum_outputs(0)
                            sum_outputs(1)
                    if s < PROJ_HALVES:
                        cut_lo(dve, 2 * n0 + s + CUT_SLOTS)
                sum_outputs(2)
                variance(3 * layer + 1, 3 * TT)
                inverse_root(3 * layer + 1, rstd[:, 0:3 * TT], link)
                gm = await_gain(3 * layer + 1)
                for t in range(TT):
                    for i, (lo, hi) in enumerate(GROUPS):
                        ins = dve.scalar_tensor_tensor(out=h[:, t, lo:hi], in0=o_tok[:, t, lo:hi],
                                                       scalar=rstd[:, 3 * t + i:3 * t + i + 1], in1=gm[:, lo:hi],
                                                       op0=ALU.mult, op1=ALU.mult)
                        if i < 2:
                            link(ins)
                    ins.then_inc(y_ready, 1)
                copy_transposed(3 * layer + 1)
                cut_lo(dve, 2 * n0 + 31)
                for half in range(2):
                    dve.wait_ge(half_used, 2 * (n0 + 12 + 2 * half + 2))
                    for t in range(TT):
                        xs = x[:, t, half * 512:(half + 1) * 512]
                        link(dve.tensor_tensor(xs, xs, bank[2 * half + t][:, :], ALU.add))
                        gained(3 * layer + 2, t, half)
                    if half == 0:
                        for m in halves(FFN0[layer]) + halves(FFN0[layer] + 1):
                            cut_lo(dve, m)
                        copy_transposed(3 * layer + 2, (0, 1))

            def hidden(g, trip, tokens):
                n = FFN0[0 if tokens == TT else 1]
                count = TT * g if tokens == TT else TT * NG + g
                dve.wait_ge(half_used, 2 * (n + up_tile(g) + 4) + per_trip(trip, 2 * PER_FFN))
                for t in range(tokens):
                    dve.wait_ge(silu_done, count + t + 1 + per_trip(trip, NG))
                    if tokens == TT:
                        dve.scalar_tensor_tensor(out=hid[:, t, :], in0=bank[2 + t][:, :], scalar=rstd_x[:, t:t + 1],
                                                 in1=hid[:, t, :], op0=ALU.mult, op1=ALU.mult).then_inc(hid_done, 1)
                    else:
                        dve.tensor_tensor(hid[:, t, :], hid[:, t, :], bank[2 + t][:, :], ALU.mult).then_inc(hid_done, 1)

            def hid_lo(count, trip, tokens):
                for t in range(tokens):
                    dve.wait_ge(hidT_hi_done, count + t + 1 + per_trip(trip, NG))
                    dve.tensor_tensor(hidT_lo[:, t, :], bank[2 + t][:, :], hidT_hi[:, t, :].bitcast(F32), ALU.subtract
                                      ).then_inc(hidT_done, 1)

            dve.wait_ge(x_in, 16)
            dve.wait_ge(const_in, 16)
            mixer(0)
            norm_products(2, (2, 3))
            for m in range(4, 2 * PER_FFN + 4):
                if m in hid_before_cut:
                    hid_lo(TT * hid_before_cut[m], 0, TT)
                if m in mult_before_cut:
                    hidden(mult_before_cut[m], 0, TT)
                cut_lo(dve, 2 * FFN0[0] + m)
            dve.wait_ge(half_used, 2 * (FFN0[0] + PER_FFN))
            for t in range(TT):
                for half in range(2):
                    xs = x[:, t, half * 512:(half + 1) * 512]
                    link(dve.tensor_tensor(xs, xs, bank[4 + 2 * t + half][:, :], ALU.add))
                    gained(3, t, half)
            norm_products(3, range(4))
            mixer(1)
            norm_products(5, (2, 3), behind=[2 * FFN0[1] + m for m in (4, 5)])

            dve.wait_ge(logits_done, 1)
            dve.tensor_copy(expert_rows, bank[4][0:2 * NE, 0:S]).then_inc(logits_copied, 1)
            dve.wait_ge(router_done, 1)
            by_part = bank[5][:, 0:TT * 2 * NE].rearrange("p (t u e) -> p t u e", t=TT, u=2)
            link(dve.tensor_copy(lg, by_part[:, :, 0, :]))
            link(dve.tensor_tensor(lg, lg, by_part[:, :, 1, :], ALU.add))
            for t in range(TT):
                link(dve.max(top[:, t, :], lg[:, t, :]))
                link(dve.max_index(idx8[:, t, :], top[:, t, :], lg[:, t, :]))
            link(dve.tensor_copy(idf, idx8[:, :, :]))
            link(dve.tensor_tensor(dz, top[:, :, 1], top[:, :, 0], ALU.subtract))
            dve.tensor_tensor(dz, dz, rstd_x, ALU.mult).then_inc(top_ready, 1)
            for t in range(TT):
                link(dve.tensor_scalar(pick0[:, t, :], iota[:, 0:NE], idf[:, t, 0:1], None, ALU.is_equal))
                link(dve.tensor_scalar(pick1[:, t, :], iota[:, 0:NE], idf[:, t, 1:2], None, ALU.is_equal))
            dve.tensor_tensor(mask, pick0, pick1, ALU.add).then_inc(mask_ready, 1)
            dve.wait_ge(mask_ready, 1)
            dve.wait_ge(pos_done, 1)
            link(dve.scalar_tensor_tensor(out=pos, in0=bank[7][:, 0:TT * NE].rearrange("p (t e) -> p t e", t=TT),
                                          scalar=1.0, in1=mask, op0=ALU.add, op1=ALU.mult))

            def gates_and_counts():
                dve.wait_ge(z_ready, 1)
                link(dve.tensor_scalar(den, z, 1.0, None, ALU.add))
                link(dve.reciprocal(g0, den))
                link(dve.tensor_tensor(g1, z, g0, ALU.mult))
                for t in range(TT):
                    link(dve.tensor_scalar(gate[:, t, :], pick0[:, t, :], g0[:, t:t + 1], None, ALU.mult))
                    link(dve.scalar_tensor_tensor(out=gate[:, t, :], in0=pick1[:, t, :], scalar=g1[:, t:t + 1],
                                                  in1=gate[:, t, :], op0=ALU.mult, op1=ALU.add))
                link(dve.tensor_copy(counts[0:1, 0:NE], bank[6][0:1, 0:NE]))
                link(dve.tensor_reduce(cnt_f[0:1, 0:1], bank[6][0:1, 0:NE], AX, ALU.max))
                dve.tensor_copy(counts[0:1, NE:NE + 1], cnt_f[0:1, 0:1]).then_inc(counts_ready, 1)

            def experts(pass_no, link):
                if pass_no:
                    link(dve.tensor_scalar(pos, pos, float(-CAP), None, ALU.add))
                for e0, e1 in ((0, 1), (1, NE)):
                    for t in range(TT):
                        dve.tensor_tensor(pick[:, e0:e1, t, :], place.unsqueeze(1).to_broadcast([P, e1 - e0, CAP]),
                                          pos[:, t, e0:e1].unsqueeze(2).to_broadcast([P, e1 - e0, CAP]), ALU.is_equal
                                          ).then_inc(pick_ready, 1)
                dve.memset(spread, 0.0).then_inc(spread_ready, 1)
                for half in range(2):
                    dve.memset(y_sb[:, half * 512:(half + 1) * 512], 0.0).then_inc(y_copied, 1)
                if not pass_no:
                    cut_lo(dve, 2 * FFN0[1] + 6)
                else:
                    for m in range(CUT_SLOTS):
                        cut_lo(dve, 2 * FFN0[1] + m, moe_trip(pass_no, 0))

                def gathered_lo(trip):
                    for half in range(2):
                        dve.wait_ge(hg_hi_done, per_trip(trip, 2) + half + 1)
                        dve.tensor_tensor(hg_lo[:, half * 4:half * 4 + 4, :],
                                          bank[4 + half][:, :].rearrange("p (k c) -> p k c", k=4),
                                          hg_hi[:, half * 4:half * 4 + 4, :].bitcast(F32), ALU.subtract
                                          ).then_inc(hg_ready, 1)

                def add_scattered(i):
                    for item in range(4):
                        t, half = item // 2, item % 2
                        dve.wait_ge(scatter_done, 4 * i + item + 1)
                        xs = x[:, t, half * 512:(half + 1) * 512]
                        dve.tensor_tensor(xs, xs, bank[SCATTER_BANKS[item]][:, :], ALU.add).then_inc(scatter_added, 1)

                def expert(e, last):
                    trip = moe_trip(pass_no, e)
                    i = e + (NE + 1) * pass_no
                    for m in range(CUT_SLOTS, 2 * PER_FFN + CUT_SLOTS):
                        if m in hid_before_cut:
                            hid_lo(TT * NG + hid_before_cut[m], trip, 1)
                            if hid_before_cut[m] == NG - 1 and not last:
                                gathered_lo(trip + 1)
                        if m in mult_before_cut:
                            hidden(mult_before_cut[m], trip, 1)
                        if m == 2 * (SCATTER + 1) + CUT_SLOTS:
                            add_scattered(i)
                        if m == 2 * SPREAD - CUT_SLOTS:
                            for t in range(TT):
                                dve.tensor_scalar(
                                    gated[:, t, :], pick[:, bass.ds(e, 1), t, :].rearrange("p e c -> p (e c)"),
                                    gate[:, t, bass.ds(e, 1)], None, ALU.mult).then_inc(gated_ready, 1)
                        if m == 2 * (SPREAD + 1) + CUT_SLOTS:
                            dve.wait_ge(spread_done, trip + 1)
                            dve.tensor_copy(spread, bank[1][:, 0:S]).then_inc(spread_ready, 1)
                        if not (last and m >= 2 * PER_FFN):
                            cut_lo(dve, 2 * FFN0[1] + m, trip)

                gathered_lo(moe_trip(pass_no, 0))
                if not pass_no:
                    gates_and_counts()
                with dve.Fori(0, NE - 1) as e:
                    expert(e, False)
                expert(NE - 1, True)
                add_scattered((NE + 1) * pass_no + NE)

            experts(0, link)
            dve.wait_ge(scatter_added, 4 * (NE + 1))
            most = dve.value_load(counts[0:1, NE:NE + 1], min_val=0, max_val=S)
            with dve.If(most > CAP):
                experts(1, linker(dve, dve_chain_pass))
                dve.wait_ge(scatter_added, 8 * (NE + 1))
                dve.nop()
            final_norm(linker(dve, dve_chain_end))

        @block.tensor
        def _(pe):
            def transpose_tokens(stage, ready, value, step, chunks=range(KD)):
                for t in range(TT):
                    pe.wait_ge(ready, value + step * (t + 1))
                    for k in chunks:
                        c0 = (k % 2) * S + t * P
                        ins = pe.transpose(turned(stage, k // 2)[:, c0:c0 + P], h[:, t, k * P:(k + 1) * P], ident)
                        if t == TT - 1 and k % 2 == 1:
                            ins.then_inc(tr_done, 1)

            def await_hT(stage):
                pe.wait_ge(hT_done, 4 * stage + 4)

            def await_cut(m, trip=0):
                pe.wait_ge(cut_done, m + 1 + per_trip(trip, 2 * PER_FFN))

            def product(out, a_hi, a_lo, m, sl, first, last):
                hi, lo = w_hi[:, m % CUT_SLOTS, sl], w_lo[:, m % CUT_SLOTS, sl]
                pe.matmul(out, a_hi, hi, start=first, stop=False)
                pe.matmul(out, a_hi, lo, start=False, stop=False)
                return pe.matmul(out, a_lo, hi, start=False, stop=last)

            def half_product(m, kk0, a_hi, a_lo, banks, trip=0):
                await_cut(m, trip)
                for t in range(len(banks)):
                    for k in range(KT // 2):
                        kk = kk0 + k
                        ins = product(banks[t][:, :], a_hi[:, kk, t * P:(t + 1) * P],
                                      a_lo[:, kk, t * P:(t + 1) * P], m, slice(k * WIDE, (k + 1) * WIDE),
                                      kk == 0, kk == KD - 1)
                ins.then_inc(half_used, 1)

            def d_product(n, half, a_hi, a_lo, banks, trip=0, stage=None):
                for u, m in enumerate(halves(n)):
                    if stage is not None:
                        pe.wait_ge(hT_done, 4 * stage + 2 * half + u + 1)
                    half_product(m, half * KT + u * (KT // 2), a_hi, a_lo, banks, trip)


            def mixer(layer):
                n0 = MIX0[layer]
                transpose_tokens(3 * layer, h_ready, 8 * layer, 2)

                def forget():
                    pe.wait_ge(wf_cut_done, layer + 1)
                    await_hT(3 * layer)
                    for t in range(TT):
                        for k in range(KD):
                            for part in (hT_hi, hT_lo):
                                ins = pe.matmul(bank[5][:, t * 2 * H_FOX:(t + 1) * 2 * H_FOX],
                                                part[:, k, t * P:(t + 1) * P],
                                                wf_cut[:, k, :, :].rearrange("p u h -> p (u h)"),
                                                start=(k == 0 and part is hT_hi), stop=(k == KD - 1 and part is hT_lo))
                    ins.then_inc(forget_tok_done, 1)

                def turn_forget():
                    pe.wait_ge(forget_tok_ready, layer + 1)
                    for t in range(TT):
                        ins = pe.transpose(bank[4][0:H_FOX, t * P:(t + 1) * P], forget_tok[:, t, :], ident)
                    ins.then_inc(forget_done, 1)

                def bias():
                    pe.wait_ge(c_ready, layer + 1)
                    for t in range(TT):
                        pe.transpose(bank[4][:, t * H_FOX:(t + 1) * H_FOX], fox[:, 0, t * P:(t + 1) * P],
                                     ident[0:H_FOX, 0:H_FOX])
                    for hh in range(H_FOX):
                        ins = pe.matmul(bank[5 + hh // 2][:, (hh % 2) * S:(hh % 2 + 1) * S],
                                        const[0:H_FOX, C_SEL + hh * P:C_SEL + (hh + 1) * P], fox[:, 1, :],
                                        start=True, stop=True)
                    ins.then_inc(bias_done, 1)

                def turn(b):
                    if b:
                        pe.wait_ge(rope_by_dve, 3 * layer + b)
                        pe.wait_ge(rope_by_pool, 3 * layer + b)
                        pe.wait_ge(logits_ready, NH * layer + HB * b)
                    for which in range(2):
                        for cc in range(2):
                            for t in range(TT):
                                c0 = which * D + (2 * b + cc) * P
                                ins = pe.transpose(bank[2 + which][:, cc * S + t * P:cc * S + (t + 1) * P],
                                                   qkv[:, t, c0:c0 + P], ident)
                        ins.then_inc(qk_tr_done, 1)

                def scores(hh):
                    if hh % HB == 0:
                        pe.wait_ge(qkT_by_act, 4 * layer + hh // HB + 1)
                        pe.wait_ge(qkT_by_dve, 4 * layer + hh // HB + 1)
                    if hh >= 2:
                        pe.wait_ge(logits_ready, NH * layer + hh - 1)
                    c, b = hh // 2, HD * (hh % 2)
                    q, k = qkT[b:b + HD, c, :], qkT[b:b + HD, KD + c, :]
                    out = bank[2 + hh % 2]
                    pe.matmul(out[:, 0:P], q[:, 0:P], k[:, 0:P], start=True, stop=True)
                    pe.matmul(out[:, P:TRI], q[:, P:S], k, start=True, stop=True).then_inc(scores_done, 1)

                def transpose_probs(hh):
                    if hh == 0:
                        pe.wait_ge(bias_ready, 2 * layer + 1)
                    if hh < H_FOX + H_MOBA:
                        pe.wait_ge(exp_done, NH * layer + hh + 1)
                    else:
                        pe.wait_ge(weighted, (NH - H_FOX - H_MOBA) * layer + hh - H_FOX - H_MOBA + 1)
                    if hh >= 2:
                        pe.wait_ge(probsT_ready, NH * layer + hh - 1)
                    for blk in range(3):
                        ins = pe.transpose(bank[4 + hh % 2][:, blk * P:(blk + 1) * P],
                                           probs[:, hh % 2, blk * P:(blk + 1) * P], ident)
                    ins.then_inc(probs_tr_done, 1)

                def values(hh):
                    q4 = hh // 4
                    if hh == 0:
                        pe.wait_ge(bias_ready, 2 * layer + 2)
                    if hh % 4 == 0 and q4 >= 2:
                        pe.wait_ge(o_ready, 4 * layer + q4 - 1)
                    pe.wait_ge(probsT_ready, NH * layer + hh + 1)
                    pT = probsT_of(hh)
                    v = [qkv[:, t, 2 * D + hh * HD:2 * D + (hh + 1) * HD] for t in range(TT)]
                    c0 = (hh % 4) * HD
                    out = bank[6 + q4 % 2]
                    pe.matmul(out[:, c0:c0 + HD], pT[:, 0:P], v[0], start=True, stop=True)
                    pe.matmul(out[:, S + c0:S + c0 + HD], pT[:, P:2 * P], v[0], start=True, stop=False)
                    pe.matmul(out[:, S + c0:S + c0 + HD], pT[:, 2 * P:TRI], v[1], start=False, stop=True
                              ).then_inc(pv_done, 1)

                for s in range(max(STEPS) + 1):
                    if s % 4 == 0 and 0 < s <= PROJ_HALVES:
                        pe.wait_ge(proj_by_act, 6 * layer + s // 4)
                        pe.wait_ge(proj_by_dve, 6 * layer + s // 4)
                    if s < PROJ_HALVES:
                        if s < 4:
                            pe.wait_ge(hT_done, 4 * 3 * layer + s + 1)
                        half_product(2 * n0 + s, (s % 4) * (KT // 2), hT_hi, hT_lo, [bank[t] for t in range(TT)])
                    for kind, i in STEPS.get(s, ()):
                        if kind == "forget":
                            forget()
                        elif kind == "turn_forget":
                            turn_forget()
                        elif kind == "bias":
                            bias()
                        elif kind == "turn":
                            turn(i)
                        elif kind == "scores":
                            scores(i)
                        elif kind == "probs":
                            transpose_probs(i)
                        else:
                            values(i)
                transpose_tokens(3 * layer + 1, y_ready, 2 * layer, 1)
                for c in range(D // WIDE):
                    for half in range(2):
                        d_product(n0 + 12 + 2 * c + half, half, hT_hi, hT_lo, [bank[2 * c + t] for t in range(TT)],
                                  stage=(None if c else 3 * layer + 1))
                        if c == 1 and half == 0:
                            transpose_tokens(3 * layer + 2, h_ready, 8 * layer + 4, 1, range(KT))

            def swiglu(n0, trip, tokens, a_hi, a_lo, y_banks, behind):
                count = 0 if tokens == TT else TT * NG

                def transpose_hid(g):
                    for t in range(tokens):
                        pe.wait_ge(hid_done, count + tokens * g + t + 1 + per_trip(trip, NG))
                        for c in range(CH):
                            ins = pe.transpose(bank[2 + t][:, c * P:(c + 1) * P], hid[:, t, c * P:(c + 1) * P], ident)
                        ins.then_inc(hid_tr_done, 1)

                for j, (kind, g, half) in enumerate(ffn_order()):
                    n = n0 + j
                    if kind == "w1" and half == 0 and g:
                        pe.wait_ge(silu_done, count + tokens * g + per_trip(trip, NG))
                    if kind == "w3" and half == 0 and g:
                        pe.wait_ge(hidT_done, count + tokens * g + per_trip(trip, NG))
                    if kind == "w2":
                        if half == 0:
                            pe.wait_ge(hidT_done, count + tokens * (g + 1) + per_trip(trip, NG))
                        for c, m in enumerate(halves(n)):
                            await_cut(m, trip)
                            cc = CT * half + c
                            for t in range(tokens):
                                for out in range(2):
                                    ins = product(y_banks[2 * t + out][:, :], hidT_hi[:, t, cc * P:(cc + 1) * P],
                                                  hidT_lo[:, t, cc * P:(cc + 1) * P], m,
                                                  slice(out * WIDE, (out + 1) * WIDE),
                                                  g == 0 and cc == 0, g == NG - 1 and cc == CH - 1)
                            ins.then_inc(half_used, 1)
                    else:
                        b0 = 0 if kind == "w1" else 2
                        d_product(n, half, a_hi, a_lo, [bank[b0 + t] for t in range(tokens)], trip,
                                  stage=(2 if tokens == TT and j < 2 else None))
                    if kind == "w1" and half == 0 and g:
                        transpose_hid(g - 1)
                    if j == down_tile(NG - 2) + 1:
                        transpose_hid(NG - 1)
                    if j in behind:
                        behind[j]()

            pe.wait_ge(const_in, 16)
            mixer(0)
            swiglu(FFN0[0], 0, TT, hT_hi, hT_lo, bank[4:8],
                   {0: lambda: transpose_tokens(2, h_ready, 6, 1, range(KT, KD))})
            mixer(1)
            transpose_tokens(5, h_ready, 14, 1, range(KT, KD))
            await_hT(5)
            pe.wait_ge(wr_cut_done, 1)
            for k in range(KD):
                for part in (hT_hi, hT_lo):
                    ins = pe.matmul(bank[4][0:2 * NE, 0:S], wr_cut[:, k, :, :].rearrange("p u e -> p (u e)"),
                                    part[:, k, :], start=(k == 0 and part is hT_hi),
                                    stop=(k == KD - 1 and part is hT_lo))
            ins.then_inc(logits_done, 1)
            pe.wait_ge(logits_copied, 1)
            for t in range(TT):
                ins = pe.transpose(bank[5][:, t * 2 * NE:(t + 1) * 2 * NE], expert_rows[:, t * P:(t + 1) * P],
                                   ident[0:2 * NE, 0:2 * NE])
            ins.then_inc(router_done, 1)
            pe.wait_ge(mask_ready, 1)
            pe.matmul(bank[7][:, 0:NE], before, mask[:, 0, :], start=True, stop=True)
            pe.matmul(bank[7][:, NE:2 * NE], ones, mask[:, 0, :], start=True, stop=False)
            pe.matmul(bank[7][:, NE:2 * NE], before, mask[:, 1, :], start=False, stop=True)
            pe.matmul(bank[6][0:1, 0:NE], ones[:, 0:1], mask[:, 0, :], start=True, stop=False)
            pe.matmul(bank[6][0:1, 0:NE], ones[:, 0:1], mask[:, 1, :], start=False, stop=True).then_inc(pos_done, 1)

            pe.wait_ge(h_scaled, TT)

            def gather(e):
                for half in range(2):
                    for k in range(4):
                        for t in range(TT):
                            rows = pick[:, bass.ds(e, 1), t, :].rearrange("p e c -> p (e c)")
                            kk = half * 4 + k
                            ins = pe.matmul(bank[4 + half][:, k * CAP:(k + 1) * CAP], h[:, t, kk * P:(kk + 1) * P],
                                            rows, start=(t == 0), stop=(t == TT - 1))
                    ins.then_inc(gather_done, 1)

            def scatter(i):
                pe.wait_ge(spread_ready, i + 1)
                pe.wait_ge(y_copied, 2 * i + 2)
                for item in range(4):
                    t, half = item // 2, item % 2
                    pe.matmul(bank[SCATTER_BANKS[item]][:, :], spread[:, t * P:(t + 1) * P],
                              y_sb[:, half * 512:(half + 1) * 512], start=True, stop=True).then_inc(scatter_done, 1)

            def expert(pass_no, e, last):
                trip = moe_trip(pass_no, e)
                i = e + (NE + 1) * pass_no
                pe.wait_ge(hg_ready, per_trip(trip, 2) + 2)

                def spread_gates():
                    pe.wait_ge(gated_ready, per_trip(trip, 2) + 2)
                    pe.wait_ge(scatter_added, 4 * i + 4)
                    for t in range(TT):
                        ins = pe.transpose(bank[1][:, t * P:(t + 1) * P], gated[:, t, :], ident)
                    ins.then_inc(spread_done, 1)

                def next_gather():
                    pe.wait_ge(spread_ready, i + 2)
                    gather(e + 1)

                behind = {SCATTER: lambda: scatter(i), SPREAD: spread_gates}
                if not last:
                    behind[down_tile(NG - 2) + 1] = next_gather
                swiglu(FFN0[1], trip, 1, hg_hi, hg_lo, bank[6:8], behind)

            def experts(pass_no):
                pe.wait_ge(pick_ready, 2 * TT * pass_no + TT)
                gather(0)
                pe.wait_ge(pick_ready, 2 * TT * pass_no + 2 * TT)
                with pe.Fori(0, NE - 1) as e:
                    expert(pass_no, e, False)
                expert(pass_no, NE - 1, True)
                scatter((NE + 1) * pass_no + NE)

            experts(0)
            pe.wait_ge(counts_ready, 1)
            most = pe.value_load(counts[0:1, NE:NE + 1], min_val=0, max_val=S)
            with pe.If(most > CAP):
                experts(1)
                pe.nop()


NAMES = ["x"] + [f"l{l}_{n}" for l in range(2) for n in ("norm_mix", "w_in", "b_f", "mix_gain", "w_out", "norm_ffn")] + [
    "l0_w1", "l0_w3", "l0_w2", "l1_w_router", "l1_we1", "l1_we3", "l1_we2", "final_norm"]


def constants():
    import numpy as np
    c = np.zeros((P, C_END), np.float32)
    r = np.arange(P)
    c[:, C_ID:C_ID + P] = np.eye(P)
    c[:, C_LT:C_LT + P] = r[:, None] < r[None, :]
    c[:, C_ONE:C_ONE + P] = 1.0
    c[:, C_IOTA:C_IOTA + P + 1] = np.arange(P + 1)[None, :]
    for j, (q0, k0) in enumerate(((0, 0), (P, 0), (P, P))):
        dist = (q0 + r[:, None]) - (k0 + r[None, :])
        causal = dist >= 0
        times = sum(((dist % dil == 0) & causal & (dist <= win // dil * dil)).astype(int)
                    for win, dil in ((128, 1), (512, 4), (2048, 16)))
        sl = slice(j * P, (j + 1) * P)
        c[:, C_CAUSAL:C_CAUSAL + TRI][:, sl] = np.where(causal, 0.0, -1e30)
        c[:, C_UNION:C_UNION + TRI][:, sl] = np.where(times > 0, 0.0, -1e30)
        c[:, C_MULT:C_MULT + TRI][:, sl] = times
    inv = np.float32(500000.0) ** (-np.arange(0, ROT, 2, dtype=np.float32) / np.float32(ROT))
    ang = np.arange(S, dtype=np.float32)[:, None] * inv[None, :].astype(np.float32)
    for t in range(TT):
        c[:, C_COS + t * HALF:C_COS + (t + 1) * HALF] = np.cos(ang[t * P:(t + 1) * P])
        c[:, C_SIN + t * HALF:C_SIN + (t + 1) * HALF] = np.sin(ang[t * P:(t + 1) * P])
    for hh in range(H_FOX):
        c[hh, C_SEL + hh * P:C_SEL + (hh + 1) * P] = 1.0
    return c


def kernel(**inputs):
    import numpy as np
    import concourse.bacc as bacc
    from concourse.bass_utils import run_bass_kernel_spmd

    nc = bacc.Bacc("TRN2", target_bir_lowering=False, num_devices=1)
    arrays, args = {}, {}
    given = {name: np.ascontiguousarray(inputs[name]) for name in NAMES}
    given["const"] = constants()
    for name, v in given.items():
        arrays[f"in_{name}"] = v
        args[name] = nc.dram_tensor(f"in_{name}", v.shape, mybir.dt.from_np(v.dtype), kind="ExternalInput").ap()
    out = nc.dram_tensor("out", (1, S, D), F32, kind="ExternalOutput").ap()
    hybrid_trunk(nc, args, out)
    r = run_bass_kernel_spmd(nc, [arrays], core_ids=[0])
    return r.results[0]["out"]
```
